# Optimizing a Trainium2 kernel written in Bass

```python
import jax, jax.numpy as jnp
from jax import lax
import numpy as np

'''Two layers of a bidirectional hybrid encoder trunk with parallel head groups.

Each layer: sandwich-RMSNorm token-mixing sub-layer where ONE combined input projection
feeds two parallel head groups (multi-scale centred pooling mixer, 2-D neighbourhood
attention over a ROWS x GRID_W token grid), their outputs concatenated into ONE output
projection; then a sandwich-RMSNorm channel mixer (dense SwiGLU on even layers,
top-2-of-8 expert SwiGLU on odd layers).
Input x: (BATCH, SEQ, D_MODEL) float32. Output: (BATCH, SEQ, D_MODEL).
'''

D_MODEL = 1024
BATCH = 1
SEQ = 256
DEPTH = 2

D_MIX = D_MODEL
D_POOL = D_MIX // 2
POOL_WINDOWS = (2, 4, 8, 16)
N_POOL_GROUPS = len(POOL_WINDOWS)
POOL_GROUP_DIM = D_POOL // N_POOL_GROUPS
D_ATTN = D_MIX - D_POOL
NA_HEAD_DIM = 32
NA_HEADS = D_ATTN // NA_HEAD_DIM
D_IN = D_POOL + 3 * D_ATTN
GRID_W = 64
NA_KH_MAX = 8
NA_KW = 16
D_FF = 4 * D_MODEL
N_EXPERTS = 8
TOP_K = 2
D_FF_EXPERT = (7 * D_MODEL) // 2
MOE_BLOCK = 256
RMS_EPS = 1e-6
N_DENSE = (DEPTH + 1) // 2
N_MOE = DEPTH // 2

kernel_name = 'hybrid_pool_natten_moe_encoder'

def rmsnorm(x, g):
    xf = x.astype(jnp.float32)
    y = xf * lax.rsqrt(jnp.mean(xf * xf, axis=-1, keepdims=True) + RMS_EPS)
    return (y * g.astype(jnp.float32)).astype(x.dtype)

def pool_mixer(u, pool_w, pool_scale):
    S = u.shape[1]
    uf = u.astype(jnp.float32)
    cs = jnp.concatenate([jnp.zeros_like(uf[:, :1]), jnp.cumsum(uf, axis=1)], axis=1)
    t = np.arange(S)
    outs = []
    for g, w in enumerate(POOL_WINDOWS):
        c_lo, c_hi = g * POOL_GROUP_DIM, (g + 1) * POOL_GROUP_DIM
        lo = np.clip(t - w // 2, 0, S)
        hi = np.clip(t + w - w // 2, 0, S)
        csg = cs[:, :, c_lo:c_hi]
        win_mean = (csg[:, hi] - csg[:, lo]) / (hi - lo).astype(np.float32)[None, :, None]
        delta = (win_mean - uf[:, :, c_lo:c_hi]).astype(u.dtype)
        outs.append(jnp.einsum('bsc,cd->bsd', delta, pool_w[g]))
    return jnp.concatenate(outs, axis=-1) * pool_scale

def neighbourhood_attention(q, k, v, rpb):
    B, S = q.shape[0], q.shape[1]
    rows = S // GRID_W
    kh = min(NA_KH_MAX, rows)
    qg = (q * (NA_HEAD_DIM ** -0.5)).reshape(B, rows, GRID_W, NA_HEADS, NA_HEAD_DIM)
    kg = k.reshape(B, rows, GRID_W, NA_HEADS, NA_HEAD_DIM)
    vg = v.reshape(B, rows, GRID_W, NA_HEADS, NA_HEAD_DIM)
    cols = np.arange(GRID_W)
    c0 = np.clip(cols - NA_KW // 2, 0, GRID_W - NA_KW)
    col_idx = c0[:, None] + np.arange(NA_KW)[None, :]
    dc = col_idx - cols[:, None] + (NA_KW - 1)

    def one_row(r):
        r0 = jnp.clip(r - kh // 2, 0, rows - kh)
        k_rows = lax.dynamic_slice_in_dim(kg, r0, kh, axis=1)
        v_rows = lax.dynamic_slice_in_dim(vg, r0, kh, axis=1)
        k_nb = k_rows[:, :, col_idx]
        v_nb = v_rows[:, :, col_idx]
        q_row = lax.dynamic_index_in_dim(qg, r, axis=1, keepdims=False)
        s = jnp.einsum('bchd,bicjhd->bhcij', q_row, k_nb, preferred_element_type=jnp.float32)
        dr = r0 + jnp.arange(kh) - r + (NA_KH_MAX - 1)
        bias = rpb[:, dr[:, None, None], dc[None, :, :]]
        s = s + jnp.transpose(bias, (0, 2, 1, 3)).astype(jnp.float32)[None]
        p = jax.nn.softmax(s.reshape(B, NA_HEADS, GRID_W, kh * NA_KW), axis=-1)
        p = p.reshape(B, NA_HEADS, GRID_W, kh, NA_KW).astype(v.dtype)
        return jnp.einsum('bhcij,bicjhd->bchd', p, v_nb)

    out = lax.map(one_row, jnp.arange(rows))
    return jnp.transpose(out, (1, 0, 2, 3, 4)).reshape(B, S, D_ATTN)

def swiglu(x, wg, wu, wd):
    a = jnp.einsum('bsd,df->bsf', x, wg)
    b = jnp.einsum('bsd,df->bsf', x, wu)
    return jnp.einsum('bsf,fd->bsd', jax.nn.silu(a) * b, wd)

def moe_swiglu(h, w_router, w_gate, w_up, w_down):
    B, S, D = h.shape
    T = B * S
    xt = h.reshape(T, D)
    logits = jnp.einsum('td,de->te', xt, w_router, preferred_element_type=jnp.float32)
    top_logit, top_idx = lax.top_k(logits, TOP_K)
    gates = jax.nn.softmax(top_logit, axis=-1)
    A = T * TOP_K
    e_flat = top_idx.reshape(A)
    g_flat = gates.reshape(A)
    tok_flat = jnp.repeat(jnp.arange(T, dtype=jnp.int32), TOP_K)
    order = jnp.argsort(e_flat)
    e_sorted = e_flat[order]
    counts = jnp.bincount(e_flat, length=N_EXPERTS)
    padded = (counts + MOE_BLOCK - 1) // MOE_BLOCK * MOE_BLOCK
    start = jnp.cumsum(counts) - counts
    pad_end = jnp.cumsum(padded)
    pad_start = pad_end - padded
    dest = pad_start[e_sorted] + (jnp.arange(A) - start[e_sorted])
    n_blocks = (A + MOE_BLOCK - 1) // MOE_BLOCK + N_EXPERTS
    n_rows = n_blocks * MOE_BLOCK
    row_tok = jnp.zeros((n_rows,), jnp.int32).at[dest].set(tok_flat[order])
    row_gate = jnp.zeros((n_rows,), jnp.float32).at[dest].set(g_flat[order])
    block_expert = jnp.minimum(
        jnp.searchsorted(pad_end, jnp.arange(n_blocks) * MOE_BLOCK, side='right'), N_EXPERTS - 1)

    def run_block(args):
        tok, gate, e = args
        xb = xt[tok]
        a = xb @ w_gate[e]
        b = xb @ w_up[e]
        y = (jax.nn.silu(a) * b) @ w_down[e]
        return y * gate[:, None].astype(y.dtype)

    ys = lax.map(run_block, (row_tok.reshape(n_blocks, MOE_BLOCK),
                             row_gate.reshape(n_blocks, MOE_BLOCK), block_expert))
    out = jnp.zeros((T, D), h.dtype).at[row_tok].add(ys.reshape(n_rows, D).astype(h.dtype))
    return out.reshape(B, S, D)

def setup_inputs(seed: int = 0) -> dict:
    key = jax.random.key(seed)
    ks = jax.random.split(key, 17)
    f32 = jnp.float32

    def nrm(k, shape, scale):
        return jax.random.normal(k, shape, f32) * scale

    def gain(k, shape):
        return 1.0 + 0.05 * jax.random.normal(k, shape, f32)

    return {
        'x': nrm(ks[0], (BATCH, SEQ, D_MODEL), 1.0),
        'mix_norm_pre': gain(ks[1], (DEPTH, D_MODEL)),
        'mix_norm_post': gain(ks[2], (DEPTH, D_MODEL)),
        'ffn_norm_pre': gain(ks[3], (DEPTH, D_MODEL)),
        'ffn_norm_post': gain(ks[4], (DEPTH, D_MODEL)),
        'w_in': nrm(ks[5], (DEPTH, D_MODEL, D_IN), D_MODEL ** -0.5),
        'pool_w': nrm(ks[6], (DEPTH, N_POOL_GROUPS, POOL_GROUP_DIM, POOL_GROUP_DIM), POOL_GROUP_DIM ** -0.5),
        'pool_scale': gain(ks[7], (DEPTH, D_POOL)),
        'na_rpb': nrm(ks[8], (DEPTH, NA_HEADS, 2 * NA_KH_MAX - 1, 2 * NA_KW - 1), 0.1),
        'w_out': nrm(ks[9], (DEPTH, D_MIX, D_MODEL), D_MIX ** -0.5),
        'dense_w_gate': nrm(ks[10], (N_DENSE, D_MODEL, D_FF), D_MODEL ** -0.5),
        'dense_w_up': nrm(ks[11], (N_DENSE, D_MODEL, D_FF), D_MODEL ** -0.5),
        'dense_w_down': nrm(ks[12], (N_DENSE, D_FF, D_MODEL), D_FF ** -0.5),
        'moe_router': nrm(ks[13], (N_MOE, D_MODEL, N_EXPERTS), D_MODEL ** -0.5),
        'moe_w_gate': nrm(ks[14], (N_MOE, N_EXPERTS, D_MODEL, D_FF_EXPERT), D_MODEL ** -0.5),
        'moe_w_up': nrm(ks[15], (N_MOE, N_EXPERTS, D_MODEL, D_FF_EXPERT), D_MODEL ** -0.5),
        'moe_w_down': nrm(ks[16], (N_MOE, N_EXPERTS, D_FF_EXPERT, D_MODEL), D_FF_EXPERT ** -0.5),
    }

def reference(x, mix_norm_pre, mix_norm_post, ffn_norm_pre, ffn_norm_post, w_in, pool_w,
              pool_scale, na_rpb, w_out, dense_w_gate, dense_w_up, dense_w_down,
              moe_router, moe_w_gate, moe_w_up, moe_w_down):
    B, S, _ = x.shape
    h = x
    for layer in range(DEPTH):
        hn = rmsnorm(h, mix_norm_pre[layer])
        proj = jnp.einsum('bsd,de->bse', hn, w_in[layer])
        u = proj[..., :D_POOL]
        q = proj[..., D_POOL:D_POOL + D_ATTN].reshape(B, S, NA_HEADS, NA_HEAD_DIM)
        k = proj[..., D_POOL + D_ATTN:D_POOL + 2 * D_ATTN].reshape(B, S, NA_HEADS, NA_HEAD_DIM)
        v = proj[..., D_POOL + 2 * D_ATTN:].reshape(B, S, NA_HEADS, NA_HEAD_DIM)
        y_pool = pool_mixer(u, pool_w[layer], pool_scale[layer])
        y_na = neighbourhood_attention(q, k, v, na_rpb[layer])
        mix = jnp.einsum('bse,ed->bsd', jnp.concatenate([y_pool, y_na], axis=-1), w_out[layer])
        h = h + rmsnorm(mix, mix_norm_post[layer])
        hn = rmsnorm(h, ffn_norm_pre[layer])
        j = layer // 2
        if layer % 2 == 0:
            f = swiglu(hn, dense_w_gate[j], dense_w_up[j], dense_w_down[j])
        else:
            f = moe_swiglu(hn, moe_router[j], moe_w_gate[j], moe_w_up[j], moe_w_down[j])
        h = h + rmsnorm(f, ffn_norm_post[layer])
    return h


_drawn_inputs = setup_inputs


def setup_inputs(seed=0):
    import zlib

    import numpy as np

    out = dict(_drawn_inputs(seed))
    spreads = {}
    factors = {}
    for name, (base, spread) in spreads.items():
        noise = np.random.default_rng([zlib.crc32(name.encode()), seed]).standard_normal(out[name].shape)
        drawn = base * np.exp(spread * noise) if base else spread * noise
        out[name] = __import__('jax').numpy.asarray(drawn.astype(out[name].dtype))
    for name, factor in factors.items():
        out[name] = (out[name] * factor).astype(out[name].dtype)
    return out
```

```python
from contextlib import ExitStack

import concourse.bass as bass
from concourse import mybir
from concourse.alu_op_type import AluOpType as ALU

ACT = mybir.ActivationFunctionType
AX = mybir.AxisListType
F32 = mybir.dt.float32
I32 = mybir.dt.int32

P = 128
D = 1024
DT = D // P
S = 256
NT = S // P
DEPTH = 2
C4 = 512
HEADS = 16
HD = 32
ROWS, COLS = 4, 64
QC = 32
WIN = 40
WIN0 = 24
KWIN = 16
RPB_H, RPB_R = 15 * 31, 31
RW = 3 * RPB_H + 3 * RPB_R + (WIN - 1) + 8 + 1
MASKED = -1e30
EPS = 1e-6
POOL_PAD = 8
FF_TILES = 4096 // P
FE = 3584
EBLOCKS = FE // C4
EPAIRS = FE // (2 * P)
NE = 8
CAP = 80
EXTRA = 2 * S // (CAP + 1)
ITEMS = NE + EXTRA
RING = 7
MIX_LOADS = 6
DENSE_LOADS = 3 * (4096 // C4)
MOE0 = 2 * MIX_LOADS + DENSE_LOADS
PER_ITEM = 3 * EBLOCKS
GROUPS = 8

K_ID, K_TRI, K_ONE = 0, P, 2 * P
K_IOTA = 3 * P
K_MASK = K_IOTA + CAP
K_EDGE = K_MASK + 2 * WIN
K_LT = K_EDGE + 64
K_EPS = K_LT + 64
K_ALL = K_EPS + 1


def mixing_first_load(layer):
    return layer * (MIX_LOADS + DENSE_LOADS)


def hybrid_encoder(nc, x, mix_pre, mix_post, ffn_pre, ffn_post, w_in, pool_w, pool_scale, rpb,
                   w_out, d_gate, d_up, d_down, router, e_gate, e_up, e_down, consts, out):
    with ExitStack() as ctx:
        def sb(name, shape, dt=F32):
            return ctx.enter_context(nc.sbuf_tensor(name, shape, dt))

        def sem(name):
            return ctx.enter_context(nc.semaphore(name))

        ring = sb("ring", [P, RING, 8 * C4])
        h = sb("h", [P, NT, D])
        hs = sb("hs", [P, NT, D])
        hT = sb("hT", [P, DT, S])
        qT = sb("qT", [P, 4, S])
        kT = sb("kT", [P, 4, S])
        vv = sb("vv", [P, NT, C4])
        uT = sb("uT", [P, 4, S + 2 * POOL_PAD])
        win_a = sb("win_a", [P, S + 2 * POOL_PAD])
        win_b = sb("win_b", [P, S + 2 * POOL_PAD])
        yaT = sb("yaT", [P, 4, S])
        bias = sb("bias", [P, HEADS * 2 * 4 * WIN])
        prob = sb("prob", [P, 2, 4, ROWS, COLS])
        pt23 = sb("pt23", [P, 2, D])
        poolw = sb("poolw", [P, 4, P])
        gpost = sb("gpost", [P, D])
        router_sb = sb("router_sb", [P, DT, NE])
        cst = sb("cst", [P, K_ALL])
        rows = sb("rows", [40, P])
        cols = sb("cols", [P, 40])
        st = sb("st", [P, 64])
        negmax = sb("negmax", [P, 2, 4])
        sums = sb("sums", [P, 2, HEADS])
        rinv = sb("rinv", [P, 2, HEADS])
        rt = sb("rt", [P, 704])
        item_pos = sb("item_pos", [P, NT, ITEMS])
        item_gate = sb("item_gate", [P, NT, ITEMS])
        cur = sb("cur", [P, 2, NT])
        plan = sb("plan", [1, 8], I32)

        ident = cst[:, K_ID:K_ID + P]
        tri = cst[:, K_TRI:K_TRI + P]
        ones = cst[:, K_ONE:K_ONE + P]
        iota = cst[:, K_IOTA:K_IOTA + CAP]
        mask = cst[:, K_MASK:K_MASK + 2 * WIN].rearrange("p (b j) -> p b j", b=2)
        edge = cst[:, K_EDGE:K_EDGE + 64].rearrange("p (g s e) -> p g s e", g=4, s=2)
        before = cst[:, K_LT:K_LT + 64].rearrange("p (e f) -> p e f", e=NE)

        def query_order(ap):
            v = ap.rearrange("p (r b c) -> p r b c", b=2, r=ROWS)
            a = [list(d) for d in v.ap]
            return bass.AP(v.tensor, v.offset + QC - 1, a[:-1] + [[-1, QC]])

        def token_order(ap):
            v = ap.rearrange("p (r c) -> p r c", r=ROWS)
            a = [list(d) for d in v.ap]
            return bass.AP(v.tensor, v.offset + QC - 1, a[:-1] + [[-1, QC]])

        biasv = bias[:, :].rearrange("p (h b i j) -> p h b i j", h=HEADS, b=2, i=ROWS)
        rwords = pt23[:, :, :].rearrange("p a n -> p (a n)")[:, 0:RW]
        attn = qT[:, :, :].rearrange("p a n -> p (a n)").rearrange("p (b n) -> p b n", b=2)
        delta = yaT
        ypT = kT

        def pt(k):
            t = hs if k < 2 else pt23
            return t[:, k % 2, :].rearrange("p (k m q) -> p k m q", k=2, m=4)

        dhid = qT
        dsilu = vv[:, 0, :].rearrange("p (a n) -> p a n", a=2)
        facc = bias[:, 0:2 * D].rearrange("p (t n) -> p t n", t=NT)
        ynat = bias[0:CAP, 2048:3072]
        yT = bias[:, 3072:3072 + DT * CAP].rearrange("p (t n) -> p t n", t=DT)
        xT = bias[:, 3712:3712 + DT * CAP].rearrange("p (t n) -> p t n", t=DT)
        ehid = bias[:, 4352:4352 + 4 * CAP].rearrange("p (a n) -> p a n", a=2)
        esilu = bias[:, 4672:4672 + 4 * CAP].rearrange("p (a n) -> p a n", a=2)
        pick = vv[:, 0, 0:2 * CAP].rearrange("p (t n) -> p t n", t=NT)
        gpick = vv[:, 0, 2 * CAP:4 * CAP].rearrange("p (t n) -> p t n", t=NT)
        spread = vv[0:CAP, 1, 0:S]

        pa, pb, pc, pd = (ctx.enter_context(nc.psum_tensor(n, [P, 2 * C4], F32)) for n in ("pa", "pb", "pc", "pd"))

        w_landed = [sem(f"w_landed{i}") for i in range(RING)]
        cst_landed = sem("cst_landed")
        x_landed = sem("x_landed")
        rows_landed = sem("rows_landed")
        poolw_landed = sem("poolw_landed")
        gpost_landed = sem("gpost_landed")
        router_landed = sem("router_landed")
        rwords_landed = sem("rwords_landed")
        bias_part = sem("bias_part")
        cols_tp = sem("cols_tp")
        cols_ready = sem("cols_ready")
        rms_pre = sem("rms_pre")
        hs_ready = sem("hs_ready")
        hs_tp = sem("hs_tp")
        hT_dve = sem("hT_dve")
        hT_act = sem("hT_act")
        fill_done = sem("fill_done")
        fill_act = sem("fill_act")
        fill_dve = sem("fill_dve")
        qk_done = sem("qk_done")
        scored = sem("scored")
        negmax_ready = sem("negmax_ready")
        exp_done = sem("exp_done")
        tp0_done = sem("tp0_done")
        tp1_done = sem("tp1_done")
        pt_dve = sem("pt_dve")
        pt_act = sem("pt_act")
        pv_done = sem("pv_done")
        attn_ready = sem("attn_ready")
        pool_step = sem("pool_step")
        delta_ready = sem("delta_ready")
        pmix_done = sem("pmix_done")
        ypT_act = sem("ypT_act")
        ypT_dve = sem("ypT_dve")
        at_done = sem("at_done")
        yaT_act = sem("yaT_act")
        yaT_dve = sem("yaT_dve")
        sub_done = sem("sub_done")
        rms_post = sem("rms_post")
        squares = sem("squares")
        h_ready = sem("h_ready")
        dve_step = sem("dve_step")
        gu_done = sem("gu_done")
        dsilu_done = sem("dsilu_done")
        dhid_ready = sem("dhid_ready")
        down_done = sem("down_done")
        logits_done = sem("logits_done")
        lshift_ready = sem("lshift_ready")
        lexp_done = sem("lexp_done")
        sel_ready = sem("sel_ready")
        count_done = sem("count_done")
        plan_ready = sem("plan_ready")
        cur_ready = sem("cur_ready")
        pick_ready = sem("pick_ready")
        gather_done = sem("gather_done")
        spread_tp = sem("spread_tp")
        spread_ready = sem("spread_ready")
        xT_ready = sem("xT_ready")
        egu_done = sem("egu_done")
        esilu_done = sem("esilu_done")
        ehid_ready = sem("ehid_ready")
        edown_done = sem("edown_done")
        yT_dve = sem("yT_dve")
        yT_act = sem("yT_act")
        ytp_done = sem("ytp_done")
        ynat_dve = sem("ynat_dve")
        ynat_act = sem("ynat_act")
        comb_done = sem("comb_done")
        facc_done = sem("facc_done")
        out_landed = sem("out_landed")

        def slot(seq):
            return ring[:, seq % RING, :]

        def landed(eng, seq):
            eng.wait_ge(w_landed[seq % RING], 16 * (seq // RING + 1))

        def landed_item(eng, i, j):
            eng.wait_ge(w_landed[(MOE0 + j) % RING], i * (16 * PER_ITEM // RING) + 16 * ((MOE0 + j) // RING + 1))

        block = ctx.enter_context(nc.Block())

        @block.sync
        def _(sp):
            sp.dma_start(h[:, :, :], x[0].rearrange("(t p) n -> p t n", p=P)).then_inc(x_landed, 16)
            sp.dma_start(cst[:, :], consts).then_inc(cst_landed, 16)

            def wait_used(seq):
                layer, j = divmod(seq, MIX_LOADS + DENSE_LOADS)
                k, part = divmod(j - MIX_LOADS, 3)
                if j < 4:
                    sp.wait_ge(fill_done, 8 * layer + 2 * j + 2)
                elif j < MIX_LOADS:
                    sp.wait_ge(sub_done, 4 * layer + 2)
                elif part < 2:
                    sp.wait_ge(gu_done, 4 * k + 4)
                elif 4 * k + 4 < FF_TILES:
                    sp.wait_ge(down_done, 4 * k + 4)
                else:
                    sp.wait_ge(sub_done, 4)

            def load(seq, src, shape):
                if seq >= RING:
                    wait_used(seq - RING)
                dst = slot(seq).rearrange("p (t n) -> p t n", t=shape)
                sp.dma_start(dst, src).then_inc(w_landed[seq % RING], 16)

            def rows_by_tile(w):
                return w.rearrange("(t p) n -> p t n", p=P)

            for layer in range(DEPTH):
                s0 = mixing_first_load(layer)
                wi, wo = rows_by_tile(w_in[layer]), rows_by_tile(w_out[layer])
                for j, c in enumerate((1, 2, 3, 0)):
                    load(s0 + j, wi[:, :, c * C4:(c + 1) * C4], DT)
                for j in range(2):
                    load(s0 + 4 + j, wo[:, :, j * C4:(j + 1) * C4], DT)
                if layer == 0:
                    for k in range(4096 // C4):
                        cut = slice(k * C4, (k + 1) * C4)
                        load(MIX_LOADS + 3 * k, rows_by_tile(d_gate[0])[:, :, cut], DT)
                        load(MIX_LOADS + 3 * k + 1, rows_by_tile(d_up[0])[:, :, cut], DT)
                        load(MIX_LOADS + 3 * k + 2, rows_by_tile(d_down[0, cut]), 4)

            def load_item(i, expert, first, last):
                wg = e_gate[0, bass.ds(expert, 1)].rearrange("e (t p) n -> p (e t) n", p=P)
                wu = e_up[0, bass.ds(expert, 1)].rearrange("e (t p) n -> p (e t) n", p=P)
                wd = e_down[0, bass.ds(expert, 1)].rearrange("e (t p) n -> p (e t) n", p=P)
                for j in range(first, last):
                    b, part = divmod(j, 3)
                    src = (wd[:, 4 * b:4 * b + 4, :] if part == 2 else
                           (wg, wu)[part][:, :, b * C4:(b + 1) * C4])
                    if j < RING and isinstance(i, int) and i == 0:
                        wait_used(MOE0 + j - RING)
                    else:
                        old, item = (j - RING, i) if j >= RING else (j - RING + PER_ITEM, i - 1)
                        done = egu_done if old % 3 < 2 else edown_done
                        sp.wait_ge(done, item * EPAIRS + 2 * (old // 3) + 2)
                    sp.dma_start(slot(MOE0 + j).rearrange("p (t n) -> p t n", t=(DT, DT, 4)[part]), src).then_inc(
                        w_landed[(MOE0 + j) % RING], 16)

            load_item(0, 0, 0, RING)
            with sp.Fori(0, NE - 1) as e:
                load_item(e, e, RING, PER_ITEM)
                load_item(e + 1, e + 1, 0, RING)
            load_item(NE - 1, NE - 1, RING, PER_ITEM)
            sp.wait_ge(plan_ready, 1)
            extra = sp.value_load(plan[0:1, 7:8], min_val=0, max_val=EXTRA)
            with sp.Fori(0, EXTRA) as n:
                with sp.If(n < extra):
                    expert = sp.value_load(plan[0:1, bass.ds(n, 1)], min_val=0, max_val=NE - 1)
                    load_item(n + NE, expert, 0, PER_ITEM)
            for t in range(NT):
                sp.wait_ge(h_ready, 2 * 3 + t + 1)
                sp.dma_start(out[0, t * P:(t + 1) * P, :], h[:, t, :]).then_inc(out_landed, 16)
            sp.wait_ge(out_landed, 16 * NT)

        @block.gpsimd
        def _(pool):
            steps = [0]

            def link(ins):
                steps[0] += 1
                ins.then_inc(pool_step, 1)
                pool.wait_ge(pool_step, steps[0])

            def load_rwords(layer, quarter):
                first = layer * HEADS * RPB_H + 4 * quarter * RPB_H + 7 * RPB_R + RPB_R // 2 - 8
                for r in range(ROWS):
                    src = bass.AP(rpb.tensor, first - RPB_R * r - (QC - 1), [[1, QC], [1, RW]])
                    pool.dma_start(rwords[QC * r:QC * (r + 1), :], src).then_inc(rwords_landed, 16)

            pool.dma_start(rows[0:16, :], mix_pre.rearrange("l (t p) -> (l t) p", p=P)).then_inc(rows_landed, 16)
            pool.dma_start(rows[16:32, :], ffn_pre.rearrange("l (t p) -> (l t) p", p=P)).then_inc(rows_landed, 16)
            pool.dma_start(rows[32:40, :], pool_scale.rearrange("l (t p) -> (l t) p", p=P)).then_inc(rows_landed, 16)
            link(pool.memset(uT[:, :, :], 0.0))

            def build_bias(layer):
                for quarter in range(4):
                    n = 4 * layer + quarter
                    load_rwords(layer, quarter)
                    pool.wait_ge(rwords_landed, 64 * (n + 1))
                    for b in range(2):
                        words = bass.AP(pt23, rwords.offset + 8 - 8 * b,
                                        [list(rwords.ap[0]), [RPB_H, 4], [RPB_R, ROWS], [1, WIN]])
                        dst = biasv[:, 4 * quarter:4 * quarter + 4, b]
                        m = mask[:, b, :].unsqueeze(1).unsqueeze(1).broadcast_to([P, 4, ROWS, WIN])
                        ins = pool.tensor_tensor(dst, words, m, ALU.add)
                        if b == 0:
                            ins.then_inc(bias_part, 1)
                        else:
                            ins.then_inc(bias_part, 1)
                            pool.wait_ge(bias_part, 2 * (n + 1))

            def load_gpost(n):
                src = (mix_post if n % 2 == 0 else ffn_post)[n // 2]
                if n:
                    pool.wait_ge(h_ready, 2 * n)
                pool.dma_start(gpost[:, :], src.partition_broadcast(P)).then_inc(gpost_landed, 16)

            def window_means(layer):
                pool.wait_ge(fill_act, 4 * layer + 4)
                pool.wait_ge(fill_dve, 4 * layer + 4)
                for g in range(4):
                    w = 2 << g
                    src, n = uT[:, g, :], S + 2 * POOL_PAD
                    for k in range(g + 1):
                        n -= 1 << k
                        dst = (win_a, win_b)[k % 2]
                        link(pool.tensor_tensor(dst[:, 0:n], src[:, 0:n], src[:, (1 << k):(1 << k) + n], ALU.add))
                        src = dst
                    at = POOL_PAD - w // 2
                    mean = src[:, at:at + S]
                    link(pool.tensor_scalar(mean, mean, 1.0 / w, None, ALU.mult))
                    ends = bass.AP(src, mean.offset, [list(mean.ap[0]), [S - 8, 2], [1, 8]])
                    link(pool.tensor_tensor(ends, ends, edge[:, g], ALU.mult))
                    pool.tensor_tensor(delta[:, g, :], mean, uT[:, g, POOL_PAD:POOL_PAD + S],
                                       ALU.subtract).then_inc(delta_ready, 1)
                    pool.wait_ge(delta_ready, 4 * layer + g + 1)

            for layer in range(DEPTH):
                if layer:
                    pool.wait_ge(pmix_done, 2 * layer)
                pool.dma_start(poolw[:, :, :], pool_w[layer].rearrange("g c d -> c g d")).then_inc(poolw_landed, 16)
                if layer == 0:
                    pool.wait_ge(cst_landed, 16)
                    build_bias(0)
                    load_gpost(0)
                    pool.dma_start(router_sb[:, :, :], router[0].rearrange("(t p) e -> p t e", p=P)).then_inc(
                        router_landed, 16)
                window_means(layer)
                if layer == 0:
                    pool.wait_ge(pv_done, GROUPS)
                    pool.wait_ge(scored, GROUPS)
                    build_bias(1)
                load_gpost(2 * layer + 1)
                if layer == 0:
                    load_gpost(2)

        @block.tensor
        def _(pe):
            mm = pe.matmul

            def transposes(n):
                for t in range(NT):
                    pe.wait_ge(hs_ready, 2 * n + t + 1)
                    bank = (pc, pd)[t]
                    for dt in range(DT):
                        ins = pe.transpose(bank[:, dt * P:(dt + 1) * P], hs[:, t, dt * P:(dt + 1) * P], ident)
                        if dt % 4 == 3:
                            ins.then_inc(hs_tp, 1)

            def wait_hT(n):
                pe.wait_ge(hT_dve, 2 * (n + 1))
                pe.wait_ge(hT_act, 2 * (n + 1))

            def mixing(layer):
                s0 = mixing_first_load(layer)

                def fill_tile(f, ep):
                    seq = s0 + (0, 1, 2, 3)[f // 2]
                    bank = pc[:, (f % 2) * C4:(f % 2 + 1) * C4]
                    if ep % 2 == 0:
                        if f >= 2:
                            pe.wait_ge((fill_act, fill_dve)[f % 2], 4 * layer + f // 2)
                        landed(pe, seq)
                    w = slot(seq).rearrange("p (t n) -> p t n", t=DT)
                    for dt in range(DT):
                        ins = mm(bank[:, (ep % 2) * S:(ep % 2 + 1) * S], w[:, dt, ep * P:(ep + 1) * P],
                                 hT[:, dt, :], start=dt == 0, stop=dt == DT - 1)
                    return ins

                def fill_v(t, half):
                    f, seq = 4 + t, s0 + 2
                    bank = pc[:, t * C4:(t + 1) * C4]
                    if half == 0:
                        pe.wait_ge((fill_act, fill_dve)[t], 4 * layer + 2)
                        landed(pe, seq)
                    w = slot(seq).rearrange("p (t n) -> p t n", t=DT)
                    for dt in range(4 * half, 4 * half + 4):
                        ins = mm(bank, hT[:, dt, t * P:(t + 1) * P], w[:, dt, :], start=dt == 0, stop=dt == DT - 1)
                    return ins

                def scores(g):
                    b, rho = g // 4, g % 4
                    if g == 0:
                        pe.wait_ge(fill_act, 4 * layer + 2)
                        pe.wait_ge(fill_dve, 4 * layer + 2)
                    else:
                        pe.wait_ge(scored, GROUPS * layer + g)
                    rows32 = slice(HD * rho, HD * (rho + 1))
                    for m in range(4):
                        q = qT[rows32, m, b * P:(b + 1) * P]
                        k = kT[rows32, m, :].rearrange("p (r c) -> p r c", r=ROWS)[:, :, WIN0 * b:WIN0 * b + WIN]
                        ins = mm(pa[:, m * 256:m * 256 + ROWS * WIN], q, k, start=True, stop=True)
                    ins.then_inc(qk_done, 1)

                def turn(g):
                    pe.wait_ge(exp_done, GROUPS * layer + g + 1)
                    if g or layer:
                        pe.wait_ge(pt_dve, GROUPS * layer + g)
                        pe.wait_ge(pt_act, GROUPS * layer + g)
                    for kt in range(2):
                        for m in range(4):
                            ins = pe.transpose(pb[:, kt * C4 + m * P:kt * C4 + (m + 1) * P],
                                               prob[:, g % 2, m, 2 * kt:2 * kt + 2, :].rearrange("p i j -> p (i j)"),
                                               ident)
                        ins.then_inc((tp0_done, tp1_done)[kt], 1)

                def values(g):
                    b, rho = g // 4, g % 4
                    pe.wait_ge(pt_dve, GROUPS * layer + g + 1)
                    pe.wait_ge(pt_act, GROUPS * layer + g + 1)
                    if g == 0:
                        pe.wait_ge(fill_act, 4 * layer + 3)
                        pe.wait_ge(fill_dve, 4 * layer + 3)
                    for m in range(4):
                        c = (4 * m + rho) * HD
                        for kt in range(2):
                            ins = mm(pd[:, b * C4 + c:b * C4 + c + HD], pt(g % 4)[:, kt, m, :], vv[:, kt, c:c + HD],
                                     start=kt == 0, stop=kt == 1)
                    ins.then_inc(pv_done, 1)

                def half_fill(n):
                    f, part = 4 + n // 2, n % 2
                    if f < 6:
                        ins = fill_v(f - 4, part)
                    else:
                        ins = fill_tile(f, 2 * (f % 2) + part)
                    if part == 1:
                        ins.then_inc(fill_done, 1)

                wait_hT(2 * layer)
                for f in range(4):
                    for ep in (2 * (f % 2), 2 * (f % 2) + 1):
                        ins = fill_tile(f, ep)
                    ins.then_inc(fill_done, 1)
                for g in range(GROUPS):
                    scores(g)
                    if g:
                        turn(g - 1)
                    half_fill(g)
                    if g == 4:
                        values(0)
                        values(1)
                    elif g == 5:
                        values(2)
                        values(3)
                    elif g > 5:
                        values(g - 2)
                turn(7)
                pe.wait_ge(poolw_landed, 16 * (layer + 1))
                pe.wait_ge(fill_act, 4 * layer + 4)
                pe.wait_ge(fill_dve, 4 * layer + 4)
                for g in range(4):
                    pe.wait_ge(delta_ready, 4 * layer + g + 1)
                    ins = mm(pc[:, g * S:(g + 1) * S], poolw[:, g, :], delta[:, g, :], start=True, stop=True)
                    if g % 2:
                        ins.then_inc(pmix_done, 1)
                values(6)
                values(7)
                for j in range(2):
                    landed(pe, s0 + 4 + j)
                pe.wait_ge(ypT_act, layer + 1)
                pe.wait_ge(ypT_dve, layer + 1)

                def project(src, k0):
                    for t in range(NT):
                        for et in range(4):
                            for j in range(2):
                                w = slot(s0 + 4 + j).rearrange("p (t n) -> p t n", t=DT)
                                ins = mm((pa, pb)[t][:, j * C4:(j + 1) * C4], src[:, et, t * P:(t + 1) * P],
                                         w[:, k0 + et, :], start=k0 + et == 0, stop=k0 + et == DT - 1)
                        if k0:
                            ins.then_inc(sub_done, 1)
                    return ins

                project(ypT, 0)
                for b in range(2):
                    pe.wait_ge(attn_ready, 2 * layer + b + 1)
                    for et in range(4):
                        ins = pe.transpose(pc[:, b * C4 + et * P:b * C4 + (et + 1) * P],
                                           attn[:, b, et * P:(et + 1) * P], ident)
                    ins.then_inc(at_done, 1)
                pe.wait_ge(yaT_act, layer + 1)
                pe.wait_ge(yaT_dve, layer + 1)
                project(yaT, 4)

            def dense():
                def gate_up(ft):
                    k = ft // 4
                    if ft % 4 == 0:
                        landed(pe, MIX_LOADS + 3 * k)
                        landed(pe, MIX_LOADS + 3 * k + 1)
                    if ft >= 4:
                        pe.wait_ge(dhid_ready, ft - 3)
                    bank = (pc, pd)[ft % 4 // 2][:, (ft % 2) * C4:(ft % 2 + 1) * C4]
                    for j in range(2):
                        w = slot(MIX_LOADS + 3 * k + j).rearrange("p (t n) -> p t n", t=DT)
                        for dt in range(DT):
                            ins = mm(bank[:, j * S:(j + 1) * S], w[:, dt, (ft % 4) * P:(ft % 4 + 1) * P],
                                     hT[:, dt, :], start=dt == 0, stop=dt == DT - 1)
                    ins.then_inc(gu_done, 1)

                def down(ft):
                    k = ft // 4
                    if ft % 4 == 0:
                        landed(pe, MIX_LOADS + 3 * k + 2)
                    pe.wait_ge(dhid_ready, ft + 1)
                    w = slot(MIX_LOADS + 3 * k + 2).rearrange("p (t n) -> p t n", t=4)
                    for t in range(NT):
                        for j in range(2):
                            ins = mm((pa, pb)[t][:, j * C4:(j + 1) * C4], dhid[:, ft % 4, t * P:(t + 1) * P],
                                     w[:, ft % 4, j * C4:(j + 1) * C4], start=ft == 0, stop=ft == FF_TILES - 1)
                        if ft == FF_TILES - 1:
                            ins.then_inc(sub_done, 1)
                    if ft < FF_TILES - 1:
                        ins.then_inc(down_done, 1)

                for ft in range(FF_TILES):
                    gate_up(ft)
                    if ft:
                        down(ft - 1)
                down(FF_TILES - 1)

            def routing():
                pe.wait_ge(router_landed, 16)
                for t in range(NT):
                    for dt in range(DT):
                        ins = mm(pb[:, t * NE:(t + 1) * NE], hT[:, dt, t * P:(t + 1) * P], router_sb[:, dt, :],
                                 start=dt == 0, stop=dt == DT - 1)
                ins.then_inc(logits_done, 1)
                pe.wait_ge(sel_ready, 1)
                sel = rt[:, 16:32].rearrange("p (t e) -> p t e", t=NT)
                mm(pb[:, C4:C4 + NE], tri, sel[:, 0], start=True, stop=True)
                mm(pb[:, C4 + NE:C4 + 2 * NE], ones, sel[:, 0], start=True, stop=False)
                mm(pb[:, C4 + NE:C4 + 2 * NE], tri, sel[:, 1], start=False, stop=True)
                mm(pb[:, C4 + 2 * NE:C4 + 3 * NE], ones, sel[:, 0], start=True, stop=False)
                mm(pb[:, C4 + 2 * NE:C4 + 3 * NE], ones, sel[:, 1], start=False, stop=True).then_inc(count_done, 1)

            def expert_pass(i):
                pe.wait_ge(pick_ready, i + 1)
                for dt in range(DT):
                    for t in range(NT):
                        ins = mm(pb[:, dt // 4 * C4 + dt % 4 * CAP:dt // 4 * C4 + (dt % 4 + 1) * CAP],
                                 hs[:, t, dt * P:(dt + 1) * P], pick[:, t, :], start=t == 0, stop=t == NT - 1)
                ins.then_inc(gather_done, 1)
                for t in range(NT):
                    ins = pe.transpose(pa[0:CAP, t * P:(t + 1) * P], gpick[:, t, :], ident)
                ins.then_inc(spread_tp, 1)
                pe.wait_ge(xT_ready, i + 1)

                def gate_up(p):
                    if p % 2 == 0:
                        landed_item(pe, i, 3 * (p // 2))
                        landed_item(pe, i, 3 * (p // 2) + 1)
                    pe.wait_ge(ehid_ready, i * EPAIRS + p + 1)
                    bank = pc[:, (p % 2) * C4:(p % 2 + 1) * C4]
                    for j in range(2):
                        w = slot(MOE0 + 3 * (p // 2) + j).rearrange("p (t n) -> p t n", t=DT)
                        for f in range(2):
                            c = (2 * (p % 2) + f) * P
                            for dt in range(DT):
                                ins = mm(bank[:, (2 * j + f) * CAP:(2 * j + f + 1) * CAP], w[:, dt, c:c + P],
                                         xT[:, dt, :], start=dt == 0, stop=dt == DT - 1)
                    ins.then_inc(egu_done, 1)
                    return ins

                def down(p):
                    if p % 2 == 0:
                        landed_item(pe, i, 3 * (p // 2) + 2)
                    pe.wait_ge(ehid_ready, i * EPAIRS + p + 3)
                    w = slot(MOE0 + 3 * (p // 2) + 2).rearrange("p (t n) -> p t n", t=4)
                    for f in range(2):
                        for dt in range(DT):
                            ins = mm(pd[:, dt // 4 * C4 + dt % 4 * CAP:dt // 4 * C4 + (dt % 4 + 1) * CAP],
                                     w[:, 2 * (p % 2) + f, dt * P:(dt + 1) * P],
                                     ehid[:, p % 2, f * CAP:(f + 1) * CAP],
                                     start=p == 0 and f == 0 and dt % 4 == 0, stop=p == EPAIRS - 1 and f == 1,
                                     skip_group_check=True)
                    ins.then_inc(edown_done, 1)
                    return ins

                for p in range(EPAIRS):
                    gate_up(p)
                    if p:
                        down(p - 1)
                down(EPAIRS - 1)
                pe.wait_ge(yT_dve, i + 1)
                pe.wait_ge(yT_act, i + 1)
                for dt in range(DT):
                    ins = pe.transpose(pb[0:CAP, dt * P:(dt + 1) * P], yT[:, dt, :], ident)
                ins.then_inc(ytp_done, 1)
                pe.wait_ge(spread_ready, i + 1)
                pe.wait_ge(ynat_dve, i + 1)
                pe.wait_ge(ynat_act, i + 1)
                for t in range(NT):
                    for j in range(2):
                        if t:
                            pe.wait_ge(facc_done, i * 4 + 4 + j + 1)
                        mm(pa[:, j * C4:(j + 1) * C4], spread[:, t * P:(t + 1) * P],
                           ynat[:, j * C4:(j + 1) * C4], start=True, stop=True).then_inc(comb_done, 1)

            pe.wait_ge(cst_landed, 16)
            pe.wait_ge(rows_landed, 48)
            pe.transpose(pa[:, 0:40], rows[:, :], ident[0:40, 0:40]).then_inc(cols_tp, 1)
            transposes(0)
            mixing(0)
            transposes(1)
            wait_hT(1)
            dense()
            transposes(2)
            mixing(1)
            transposes(3)
            wait_hT(3)
            routing()
            with pe.Fori(0, NE) as i:
                expert_pass(i)
            pe.wait_ge(plan_ready, 1)
            extra = pe.value_load(plan[0:1, 7:8], min_val=0, max_val=EXTRA)
            with pe.Fori(0, EXTRA) as n:
                with pe.If(n < extra):
                    expert_pass(n + NE)

        @block.scalar
        def _(act):
            sums_taken = [0]

            def rms(dst, src, c):
                sums_taken[0] += 1
                s = st[:, c:c + 1]
                act.activation(dst, src, ACT.Square, accum_out=s).then_inc(squares, 1)
                act.wait_ge(squares, sums_taken[0])
                return act.activation(s, s, ACT.Sqrt, scale=1.0 / D, bias=cst[:, K_EPS:K_EPS + 1])

            act.wait_ge(cst_landed, 16)

            def pre_norm(n):
                for t in range(NT):
                    if n == 0:
                        act.wait_ge(x_landed, 16)
                    else:
                        act.wait_ge(h_ready, 2 * (n - 1) + t + 1)
                    rms(hs[:, t, :], h[:, t, :], 2 * n + t).then_inc(rms_pre, 1)
                for t in range(NT):
                    act.wait_ge(hs_tp, 4 * n + 2 * t + 2)
                    if n == 0 and t == 0:
                        act.wait_ge(cols_ready, 1)
                    for dt in range(4, DT):
                        g = (n % 2) * 16 + (n // 2) * DT + dt
                        ins = act.activation(hT[:, dt, t * P:(t + 1) * P], (pc, pd)[t][:, dt * P:(dt + 1) * P],
                                             ACT.Copy, scale=cols[:, g:g + 1])
                    ins.then_inc(hT_act, 1)

            def post_norm(n):
                for t in range(NT):
                    act.wait_ge(sub_done, 2 * n + t + 1)
                    src = facc[:, t, :] if n == 3 else (pa, pb)[t][:, :]
                    rms(hs[:, t, :], src, 8 + 2 * n + t).then_inc(rms_post, 1)

            def mixing(layer):
                def fill_q():
                    act.wait_ge(fill_done, 8 * layer + 1)
                    for m in range(2):
                        dst = qT[:, m, :].rearrange("p (b r c) -> p r b c", b=2, r=ROWS)
                        src = query_order(pc[:, m * S:(m + 1) * S])
                        ins = act.activation(dst, src, ACT.Copy, scale=HD ** -0.5)
                    ins.then_inc(fill_act, 1)

                def fill(f, dst, scale=1.0):
                    act.wait_ge(fill_done, 8 * layer + f + 1)
                    src = pc[:, 0:C4]
                    if f != 4:
                        src = src.rearrange("p (a n) -> p a n", a=2)
                    act.activation(dst, src, ACT.Copy, scale=scale).then_inc(fill_act, 1)

                def exps(g):
                    b, rho = g // 4, g % 4
                    act.wait_ge(negmax_ready, GROUPS * layer + g + 1)
                    for m in range(4):
                        p = prob[:, g % 2, m, :, WIN0 * b:WIN0 * b + WIN]
                        hd = 4 * m + rho
                        ins = act.activation(p, p, ACT.Exp, bias=negmax[:, g % 2, m:m + 1],
                                             accum_out=sums[:, b, hd:hd + 1])
                    ins.then_inc(exp_done, 1)

                def probs_out(g):
                    act.wait_ge(tp1_done, GROUPS * layer + g + 1)
                    if g >= 4:
                        act.wait_ge(pv_done, GROUPS * layer + g - 3)
                    act.activation(pt(g % 4)[:, 1], pb[:, C4:2 * C4].rearrange("p (m q) -> p m q", m=4),
                                   ACT.Copy).then_inc(pt_act, 1)

                fill_q()
                fill(2, kT[:, 0:2, :])
                for g in range(GROUPS):
                    exps(g)
                    if g:
                        probs_out(g - 1)
                    if g == 1:
                        fill(4, vv[:, 0, :])
                    if g == 5:
                        fill(6, uT[:, 0:2, POOL_PAD:POOL_PAD + S])
                probs_out(7)
                act.wait_ge(qk_done, GROUPS * (layer + 1))
                act.wait_ge(pmix_done, 2 * layer + 1)
                for g in range(2):
                    c = 32 + 4 * layer + g
                    ins = act.activation(ypT[:, g, :], pc[:, g * S:(g + 1) * S], ACT.Copy, scale=cols[:, c:c + 1])
                ins.then_inc(ypT_act, 1)
                act.wait_ge(at_done, 2 * layer + 1)
                for et in range(4):
                    ins = act.activation(yaT[:, et, :].rearrange("p (r c) -> p r c", r=ROWS)[:, :, 0:QC],
                                         token_order(pc[:, et * P:(et + 1) * P]), ACT.Copy)
                ins.then_inc(yaT_act, 1)

            def expert_pass(i):
                act.wait_ge(spread_tp, i + 1)
                act.activation(spread, pa[0:CAP, 0:S], ACT.Copy).then_inc(spread_ready, 1)
                for p in range(EPAIRS):
                    act.wait_ge(egu_done, i * EPAIRS + p + 1)
                    act.wait_ge(ehid_ready, i * EPAIRS + p + 1)
                    act.activation(esilu[:, p % 2, :], pc[:, (p % 2) * C4:(p % 2) * C4 + 2 * CAP],
                                   ACT.Silu).then_inc(esilu_done, 1)
                act.wait_ge(edown_done, (i + 1) * EPAIRS)
                act.activation(yT[:, 4:8, :], pd[:, C4:C4 + 4 * CAP].rearrange("p (t n) -> p t n", t=4),
                               ACT.Copy).then_inc(yT_act, 1)
                act.wait_ge(ytp_done, i + 1)
                act.activation(ynat[:, C4:2 * C4], pb[0:CAP, C4:2 * C4], ACT.Copy).then_inc(ynat_act, 1)

            pre_norm(0)
            mixing(0)
            post_norm(0)
            pre_norm(1)
            for ft in range(FF_TILES):
                act.wait_ge(gu_done, ft + 1)
                if ft >= 2:
                    act.wait_ge(dhid_ready, ft - 1)
                bank = (pc, pd)[ft % 4 // 2][:, (ft % 2) * C4:(ft % 2) * C4 + S]
                act.activation(dsilu[:, ft % 2, :], bank, ACT.Silu).then_inc(dsilu_done, 1)
            post_norm(1)
            pre_norm(2)
            mixing(1)
            post_norm(2)
            pre_norm(3)
            act.wait_ge(lshift_ready, 1)
            act.activation(rt[:, 48:64], rt[:, 32:48], ACT.Exp).then_inc(lexp_done, 1)
            with act.Fori(0, NE) as i:
                expert_pass(i)
            act.wait_ge(plan_ready, 1)
            extra = act.value_load(plan[0:1, 7:8], min_val=0, max_val=EXTRA)
            with act.Fori(0, EXTRA) as n:
                with act.If(n < extra):
                    expert_pass(n + NE)
            post_norm(3)

        @block.vector
        def _(dve):
            steps = [0]

            def link(ins):
                steps[0] += 1
                ins.then_inc(dve_step, 1)
                dve.wait_ge(dve_step, steps[0])

            def rms_inverse(c):
                link(dve.reciprocal(st[:, c:c + 1], st[:, c:c + 1]))

            def pre_norm(n):
                for t in range(NT):
                    dve.wait_ge(rms_pre, 2 * n + t + 1)
                    rms_inverse(2 * n + t)
                    dve.tensor_scalar(hs[:, t, :], h[:, t, :], st[:, 2 * n + t:2 * n + t + 1], None,
                                      ALU.mult).then_inc(hs_ready, 1)
                if n == 0:
                    dve.wait_ge(cols_tp, 1)
                    dve.tensor_copy(cols[:, :], pa[:, 0:40]).then_inc(cols_ready, 1)
                    dve.wait_ge(cols_ready, 1)
                for t in range(NT):
                    dve.wait_ge(hs_tp, 4 * n + 2 * t + 1)
                    g = (n % 2) * 16 + (n // 2) * DT
                    gain = cols[:, g:g + 4].unsqueeze(2).broadcast_to([P, 4, P])
                    dve.tensor_tensor(hT[:, 0:4, t * P:(t + 1) * P],
                                      (pc, pd)[t][:, 0:C4].rearrange("p (a n) -> p a n", a=4), gain,
                                      ALU.mult).then_inc(hT_dve, 1)

            def post_norm(n):
                dve.wait_ge(gpost_landed, 16 * (n + 1))
                for t in range(NT):
                    dve.wait_ge(rms_post, 2 * n + t + 1)
                    rms_inverse(8 + 2 * n + t)
                    src = facc[:, t, :] if n == 3 else (pa, pb)[t][:, :]
                    link(dve.scalar_tensor_tensor(out=hs[:, t, :], in0=src, scalar=st[:, 8 + 2 * n + t:9 + 2 * n + t],
                                                  in1=gpost[:, :], op0=ALU.mult, op1=ALU.mult))
                    dve.tensor_tensor(h[:, t, :], h[:, t, :], hs[:, t, :], ALU.add).then_inc(h_ready, 1)

            def mixing(layer):
                def fill(f, dst):
                    dve.wait_ge(fill_done, 8 * layer + f + 1)
                    src = pc[:, C4:2 * C4]
                    if f != 5:
                        src = src.rearrange("p (a n) -> p a n", a=2)
                    dve.tensor_copy(dst, src).then_inc(fill_dve, 1)

                def fill_q():
                    dve.wait_ge(fill_done, 8 * layer + 2)
                    for m in range(2, 4):
                        dst = qT[:, m, :].rearrange("p (b r c) -> p r b c", b=2, r=ROWS)
                        src = query_order(pc[:, m * S:(m + 1) * S])
                        ins = dve.tensor_scalar(dst, src, HD ** -0.5, None, ALU.mult)
                    ins.then_inc(fill_dve, 1)

                def add_bias(g):
                    b, rho = g // 4, g % 4
                    if g == 0:
                        dve.wait_ge(bias_part, 8 * (layer + 1))
                    if g >= 2:
                        dve.wait_ge(tp1_done, GROUPS * layer + g - 1)
                    if g % 4 < 2:
                        c = WIN if b == 0 else 0
                        dve.memset(prob[:, g % 2, :, :, c:c + COLS - WIN].rearrange("p m i j -> p (m i) j"), 0.0)
                    dve.wait_ge(qk_done, GROUPS * layer + g + 1)
                    win = prob[:, g % 2, :, :, WIN0 * b:WIN0 * b + WIN]
                    sc = pa[:, :].rearrange("p (m n) -> p m n", m=4)[:, :, 0:ROWS * WIN].rearrange(
                        "p m (i j) -> p m i j", i=ROWS)
                    bs = bias[:, :].rearrange("p (m r b i j) -> p m r b i j", m=4, r=4, b=2, i=ROWS)[:, :, rho, b]
                    dve.tensor_tensor(win, sc, bs, ALU.add).then_inc(scored, 1)
                    dve.wait_ge(scored, GROUPS * layer + g + 1)
                    nm = negmax[:, g % 2, :]
                    link(dve.tensor_reduce(nm, win, AX.XY, ALU.max))
                    dve.tensor_scalar(nm, nm, -1.0, None, ALU.mult).then_inc(negmax_ready, 1)

                def probs_out(g):
                    dve.wait_ge(tp0_done, GROUPS * layer + g + 1)
                    if g >= 4:
                        dve.wait_ge(pv_done, GROUPS * layer + g - 3)
                    dve.tensor_copy(pt(g % 4)[:, 0], pb[:, 0:C4].rearrange("p (m q) -> p m q", m=4)).then_inc(
                        pt_dve, 1)

                fill_q()
                fill(3, kT[:, 2:4, :])
                for g in range(GROUPS):
                    add_bias(g)
                    if g:
                        probs_out(g - 1)
                    if g == 3:
                        fill(5, vv[:, 1, :])
                    if g == 7:
                        fill(7, uT[:, 2:4, POOL_PAD:POOL_PAD + S])
                probs_out(7)
                dve.wait_ge(pmix_done, 2 * layer + 2)
                for g in range(2, 4):
                    c = 32 + 4 * layer + g
                    ins = dve.tensor_scalar(ypT[:, g, :], pc[:, g * S:(g + 1) * S], cols[:, c:c + 1], None, ALU.mult)
                ins.then_inc(ypT_dve, 1)
                dve.wait_ge(exp_done, GROUPS * (layer + 1))
                link(dve.reciprocal(rinv[:, :, :].rearrange("p b h -> p (b h)"),
                                    sums[:, :, :].rearrange("p b h -> p (b h)")))
                for b in range(2):
                    dve.wait_ge(pv_done, GROUPS * layer + 4 * (b + 1))
                    dve.tensor_tensor(attn[:, b, :].rearrange("p (h d) -> p h d", h=HEADS),
                                      pd[:, b * C4:(b + 1) * C4].rearrange("p (h d) -> p h d", h=HEADS),
                                      rinv[:, b, :].unsqueeze(2).broadcast_to([P, HEADS, HD]),
                                      ALU.mult).then_inc(attn_ready, 1)
                dve.wait_ge(at_done, 2 * layer + 2)
                for et in range(4):
                    dst = yaT[:, et, :].rearrange("p (r c) -> p r c", r=ROWS)[:, :, QC:2 * QC]
                    ins = dve.tensor_copy(dst, token_order(pc[:, C4 + et * P:C4 + (et + 1) * P]))
                ins.then_inc(yaT_dve, 1)

            def routing():
                def f(c, n):
                    return rt[:, c:c + n]

                def te(ap):
                    return ap.rearrange("p (t e) -> p t e", t=NT)

                lg, sel, sh, ex = f(0, 16), f(16, 16), f(32, 16), f(48, 16)
                m1, den = f(64, 2), f(66, 2)
                gates = f(80, 16)
                pos = f(96, 16)
                cnt, extras, base, inc = f(112, 8), f(120, 8), f(128, 8), f(136, 8)
                rho, slots, item, tmp = f(144, 16), f(160, 16), f(176, 16), f(192, 16)
                row = f(208, 8)
                big = f(256, 128).rearrange("p (t e f) -> p t e f", t=NT, e=NE)
                big2 = f(384, 128).rearrange("p (t e f) -> p t e f", t=NT, e=NE)
                rank = f(224, 16)
                dve.wait_ge(logits_done, 1)
                link(dve.tensor_copy(lg, pb[:, 0:16]))
                other = te(lg).unsqueeze(2).broadcast_to([P, NT, NE, NE])
                own = te(lg).unsqueeze(3).broadcast_to([P, NT, NE, NE])
                lower = before.unsqueeze(1).broadcast_to([P, NT, NE, NE])
                dve.tensor_tensor(big, other, own, ALU.is_gt)
                link(dve.tensor_tensor(big2, other, own, ALU.is_equal))
                for t in range(NT):
                    ins = dve.tensor_tensor(big2[:, t], big2[:, t], before, ALU.mult)
                link(ins)
                link(dve.tensor_tensor(f(256, 128), f(256, 128), f(384, 128), ALU.add))
                dve.tensor_reduce(te(rank), big, AX.X, ALU.add)
                link(dve.tensor_reduce(m1, te(lg), AX.X, ALU.max))
                dve.tensor_scalar(sel, rank, 1.5, None, ALU.is_lt).then_inc(sel_ready, 1)
                dve.tensor_tensor(te(sh), te(lg), m1.unsqueeze(2).broadcast_to([P, NT, NE]),
                                  ALU.subtract).then_inc(lshift_ready, 1)
                dve.memset(facc[:, :, :].rearrange("p t n -> p (t n)"), 0.0).then_inc(facc_done, 4)
                dve.wait_ge(sel_ready, 1)
                dve.wait_ge(lexp_done, 1)
                link(dve.tensor_tensor(ex, ex, sel, ALU.mult))
                link(dve.tensor_reduce(den, te(ex), AX.X, ALU.add))
                link(dve.reciprocal(den, den))
                link(dve.tensor_tensor(te(gates), te(ex), den.unsqueeze(2).broadcast_to([P, NT, NE]), ALU.mult))
                dve.wait_ge(count_done, 1)
                dve.tensor_copy(cnt, pb[:, C4 + 16:C4 + 24])
                link(dve.scalar_tensor_tensor(out=pos, in0=pb[:, C4:C4 + 16], scalar=1.0, in1=sel,
                                              op0=ALU.add, op1=ALU.mult))
                link(dve.tensor_scalar(pos, pos, -1.0, None, ALU.add))
                dve.tensor_copy(item_pos[:, :, 0:NE], te(pos))
                link(dve.tensor_copy(item_gate[:, :, 0:NE], te(gates)))
                link(dve.tensor_scalar(extras, cnt, CAP + 0.5, None, ALU.is_gt))
                link(dve.tensor_scalar(rho, pos, CAP - 0.5, None, ALU.is_gt))
                k = 2
                while k * CAP < S:
                    link(dve.scalar_tensor_tensor(out=extras, in0=cnt, scalar=k * CAP + 0.5, in1=extras,
                                                  op0=ALU.is_gt, op1=ALU.add))
                    link(dve.scalar_tensor_tensor(out=rho, in0=pos, scalar=k * CAP - 0.5, in1=rho,
                                                  op0=ALU.is_gt, op1=ALU.add))
                    k += 1
                link(dve.tensor_tensor(big[:, 0], before, extras.unsqueeze(1).broadcast_to([P, NE, NE]), ALU.mult))
                link(dve.tensor_reduce(base, big[:, 0], AX.X, ALU.add))
                link(dve.tensor_tensor(inc, base, extras, ALU.add))
                link(dve.scalar_tensor_tensor(out=slots, in0=rho, scalar=-float(CAP), in1=pos,
                                              op0=ALU.mult, op1=ALU.add))
                link(dve.tensor_scalar(slots, slots, 1.0, None, ALU.add))
                link(dve.tensor_tensor(te(item), te(rho), base.unsqueeze(1).broadcast_to([P, NT, NE]), ALU.add))
                link(dve.tensor_scalar(tmp, rho, 0.5, None, ALU.is_gt))
                link(dve.tensor_tensor(item, item, tmp, ALU.mult))
                for n in range(EXTRA):
                    link(dve.scalar_tensor_tensor(out=tmp, in0=item, scalar=float(n + 1), in1=slots,
                                                  op0=ALU.is_equal, op1=ALU.mult))
                    link(dve.tensor_reduce(item_pos[:, :, NE + n], te(tmp), AX.X, ALU.add))
                    link(dve.scalar_tensor_tensor(out=tmp, in0=item, scalar=float(n + 1), in1=gates,
                                                  op0=ALU.is_equal, op1=ALU.mult))
                    link(dve.tensor_reduce(item_gate[:, :, NE + n], te(tmp), AX.X, ALU.add))
                    link(dve.tensor_scalar(tmp[:, 0:NE], inc, n + 0.5, None, ALU.is_lt))
                    link(dve.tensor_reduce(row[:, n:n + 1], tmp[:, 0:NE], AX.X, ALU.add))
                link(dve.tensor_scalar(item_pos[:, :, NE:ITEMS], item_pos[:, :, NE:ITEMS], -1.0, None, ALU.add))
                link(dve.memset(row[:, EXTRA:7], 0.0)) if EXTRA < 7 else None
                link(dve.tensor_scalar(row[:, 0:7], row[:, 0:7], float(NE - 1), None, ALU.min))
                link(dve.tensor_copy(row[:, 7:8], inc[:, 7:8]))
                dve.tensor_copy(plan[0:1, :], row[0:1, :]).then_inc(plan_ready, 1)
                dve.memset(f(248, 1), 0.0).then_inc(ehid_ready, 2)

            def expert_pass(i):
                dve.tensor_copy(cur[:, 0, :], item_pos[:, :, bass.ds(i, 1)].rearrange("p t i -> p (t i)"))
                dve.tensor_copy(cur[:, 1, :], item_gate[:, :, bass.ds(i, 1)].rearrange("p t i -> p (t i)")).then_inc(
                    cur_ready, 1)
                dve.wait_ge(cur_ready, i + 1)
                for t in range(NT):
                    dve.tensor_scalar(pick[:, t, :], iota, cur[:, 0, t:t + 1], None, ALU.is_equal)
                    ins = dve.tensor_scalar(gpick[:, t, :], iota, cur[:, 0, t:t + 1], cur[:, 1, t:t + 1],
                                            ALU.is_equal, ALU.mult)
                ins.then_inc(pick_ready, 1)
                dve.wait_ge(gather_done, i + 1)
                g = 16 + DT
                src = pb[:, :].rearrange("p (b n) -> p b n", b=2)[:, :, 0:4 * CAP].rearrange(
                    "p b (t n) -> p b t n", t=4)
                gain = cols[:, g:g + DT].rearrange("p (b t) -> p b t", b=2).unsqueeze(3).broadcast_to([P, 2, 4, CAP])
                dve.tensor_tensor(xT.rearrange("p (b t) n -> p b t n", b=2), src, gain, ALU.mult).then_inc(
                    xT_ready, 1)
                for p in range(EPAIRS):
                    dve.wait_ge(esilu_done, i * EPAIRS + p + 1)
                    if p >= 2:
                        dve.wait_ge(edown_done, i * EPAIRS + p - 1)
                    dve.tensor_tensor(ehid[:, p % 2, :], pc[:, (p % 2) * C4 + 2 * CAP:(p % 2) * C4 + 4 * CAP],
                                      esilu[:, p % 2, :], ALU.mult).then_inc(ehid_ready, 1)
                dve.wait_ge(edown_done, (i + 1) * EPAIRS)
                dve.tensor_copy(yT[:, 0:4, :], pd[:, 0:4 * CAP].rearrange("p (t n) -> p t n", t=4)).then_inc(
                    yT_dve, 1)
                dve.wait_ge(ytp_done, i + 1)
                dve.tensor_copy(ynat[:, 0:C4], pb[0:CAP, 0:C4]).then_inc(ynat_dve, 1)
                for t in range(NT):
                    for j in range(2):
                        q = facc[:, t, j * C4:(j + 1) * C4]
                        dve.wait_ge(comb_done, i * 4 + 2 * t + j + 1)
                        dve.wait_ge(facc_done, i * 4 + 2 * t + j + 1)
                        dve.tensor_tensor(q, q, pa[:, j * C4:(j + 1) * C4], ALU.add).then_inc(facc_done, 1)

            pre_norm(0)
            mixing(0)
            post_norm(0)
            pre_norm(1)
            for ft in range(FF_TILES):
                dve.wait_ge(dsilu_done, ft + 1)
                if ft >= 4:
                    dve.wait_ge(down_done, ft - 3)
                bank = (pc, pd)[ft % 4 // 2][:, (ft % 2) * C4 + S:(ft % 2 + 1) * C4]
                dve.tensor_tensor(dhid[:, ft % 4, :], bank, dsilu[:, ft % 2, :], ALU.mult).then_inc(dhid_ready, 1)
            post_norm(1)
            pre_norm(2)
            mixing(1)
            post_norm(2)
            pre_norm(3)
            routing()
            with dve.Fori(0, NE) as i:
                expert_pass(i)
            dve.wait_ge(plan_ready, 1)
            extra = dve.value_load(plan[0:1, 7:8], min_val=0, max_val=EXTRA)
            with dve.Fori(0, EXTRA) as n:
                with dve.If(n < extra):
                    expert_pass(n + NE)
            dve.memset(st[:, 32:33], 0.0).then_inc(sub_done, 2)
            post_norm(3)


_INS = ['x', 'mix_norm_pre', 'mix_norm_post', 'ffn_norm_pre', 'ffn_norm_post', 'w_in', 'pool_w', 'pool_scale',
        'na_rpb', 'w_out', 'dense_w_gate', 'dense_w_up', 'dense_w_down', 'moe_router', 'moe_w_gate', 'moe_w_up',
        'moe_w_down']


def shape_constants():
    import numpy as np
    c = np.zeros((P, K_ALL), np.float32)
    p = np.arange(P)
    c[:, K_ID:K_ID + P] = np.eye(P)
    c[:, K_TRI:K_TRI + P] = p[:, None] < p[None, :]
    c[:, K_ONE:K_ONE + P] = 1
    c[:, K_IOTA:K_IOTA + CAP] = np.arange(CAP)
    for b in range(2):
        first = np.clip(QC - 1 - p % QC + QC * b - KWIN // 2, 0, COLS - KWIN)[:, None]
        col = WIN0 * b + np.arange(WIN)[None, :]
        seen = (col >= first) & (col < first + KWIN)
        c[:, K_MASK + b * WIN:K_MASK + (b + 1) * WIN] = np.where(seen, 0, MASKED)
    t = np.concatenate([np.arange(8), np.arange(S - 8, S)])
    for g in range(4):
        w = 2 << g
        n = np.clip(t + w - w // 2, 0, S) - np.clip(t - w // 2, 0, S)
        c[:, K_EDGE + 16 * g:K_EDGE + 16 * (g + 1)] = w / n
    e = np.arange(NE)
    c[:, K_EPS] = EPS
    c[:, K_LT:K_LT + 64] = (e[None, :] < e[:, None]).reshape(-1)
    return c


def kernel(**inputs):
    import numpy as np
    import concourse.bacc as bacc
    from concourse.bass_utils import run_bass_kernel_spmd

    nc = bacc.Bacc("TRN2", target_bir_lowering=False, num_devices=1)
    arrays, args = {}, []
    for name in _INS:
        a = np.ascontiguousarray(inputs[name])
        arrays[f"in_{name}"] = a
        args.append(nc.dram_tensor(f"in_{name}", a.shape, mybir.dt.from_np(a.dtype), kind="ExternalInput").ap())
    consts = shape_constants()
    arrays["in_consts"] = consts
    args.append(nc.dram_tensor("in_consts", consts.shape, F32, kind="ExternalInput").ap())
    args.append(nc.dram_tensor("out", (1, S, D), F32, kind="ExternalOutput").ap())
    hybrid_encoder(nc, *args)
    r = run_bass_kernel_spmd(nc, [arrays], core_ids=[0])
    return r.results[0]["out"]
```

```python
from contextlib import ExitStack

import concourse.bass as bass
from concourse import mybir
from concourse.alu_op_type import AluOpType as ALU

ACT = mybir.ActivationFunctionType
AX = mybir.AxisListType
F32 = mybir.dt.float32
F32R = mybir.dt.float32r
I32 = mybir.dt.int32

P = 128
D = 1024
DT = D // P
S = 256
NT = S // P
DEPTH = 2
C4 = 512
C2 = 256
HEADS = 16
HD = 32
ROWS, COLS = 4, 64
QC = 32
WIN = 40
WIN0 = 24
KWIN = 16
RPB_H, RPB_R = 15 * 31, 31
RW = 3 * RPB_H + 3 * RPB_R + (WIN - 1) + 8 + 1
MASKED = -1e30
EPS = 1e-6
POOL_PAD = 8
FE = 3584
DBLOCKS = 4096 // C4
EBLOCKS = FE // C4
NE = 8
CAP = 80
EXTRA = 2 * S // (CAP + 1)
ITEMS = NE + EXTRA
GROUPS = 8

RING = 3
STAGE = 3
MIX_LOADS = 6
DENSE_LOADS = 3 * DBLOCKS
PER_ITEM = 3 * EBLOCKS
MOE0 = 2 * MIX_LOADS + DENSE_LOADS
assert PER_ITEM % RING == 0 and 2 * PER_ITEM % STAGE == 0 and 2 * MOE0 % STAGE == 0


def ffn_order(blocks):
    order = [("gate", 0), ("up", 0)]
    for b in range(1, blocks):
        order += [("gate", b), ("down", b - 1), ("up", b)]
    return order + [("down", blocks - 1)]


DENSE = ffn_order(DBLOCKS)
EXPERT = ffn_order(EBLOCKS)
EXPERT[-3:] = [EXPERT[-2], EXPERT[-3], EXPERT[-1]]


K_ID, K_TRI, K_ONE = 0, P, 2 * P
K_IOTA = 3 * P
K_MASK = K_IOTA + CAP
K_EDGE = K_MASK + 2 * WIN
K_LT = K_EDGE + 64
K_EPS = K_LT + 64
K_ALL = K_EPS + 1


def mixing_first_load(layer):
    return layer * (MIX_LOADS + DENSE_LOADS)


def hybrid_encoder(nc, x, mix_pre, mix_post, ffn_pre, ffn_post, w_in, pool_w, pool_scale, rpb,
                   w_out, d_gate, d_up, d_down, router, e_gate, e_up, e_down, consts, out):
    with ExitStack() as ctx:
        def sem(name):
            return ctx.enter_context(nc.semaphore(name))

        plan_top = [-(-nc.sbuf_base // 32) * 32]

        def sb(name, shape, dt=F32, over=None, skip=0):
            size = 4
            for n in shape[1:]:
                size *= n
            if over is None:
                at = plan_top[0]
                plan_top[0] += -(-size // 32) * 32
            else:
                at = addr[over] + skip
            addr[name] = at
            return nc.alloc_sbuf_tensor_at(name, shape, dt, offset=at)

        addr = {}
        ring = sb("ring", [P, RING, 8 * C4])
        w_hi = sb("w_hi", [P, STAGE, 8 * C2], F32R)
        w_lo = sb("w_lo", [P, STAGE, 8 * C2], F32R)
        h = sb("h", [P, NT, D])
        hs = sb("hs", [P, NT, D])
        hT_hi = sb("hT_hi", [P, DT, S], F32R)
        hT_lo = sb("hT_lo", [P, DT, S], F32R)
        gpre = sb("gpre", [P, D])
        gpost = sb("gpost", [P, D])
        router_sb = sb("router_sb", [P, DT, NE])
        cst = sb("cst", [P, K_ALL])
        rows = sb("rows", [8, P])
        cols = sb("cols", [P, 8])
        st = sb("st", [P, 64])
        qT = sb("qT", [P, 4, S])
        kT = sb("kT", [P, 4, S])
        vv = sb("vv", [P, NT, C4])
        uT = sb("uT", [P, 4, S + 2 * POOL_PAD])
        win_a = sb("win_a", [P, S + 2 * POOL_PAD])
        win_b = sb("win_b", [P, S + 2 * POOL_PAD])
        bias = sb("bias", [P, HEADS * 2 * ROWS * WIN])
        prob = sb("prob", [P, 2, 4, ROWS, COLS])
        pt23 = sb("pt23", [P, 2, D])
        poolw = sb("poolw", [P, 4, P])
        ypT_lo = sb("ypT_lo", [P, 4, S], F32R)
        delta = sb("delta", [P, 4, S])
        negmax = sb("negmax", [P, 2, 4])
        sums = sb("sums", [P, 2, HEADS])
        rinv = sb("rinv", [P, 2, HEADS])
        rt = sb("rt", [P, 512])
        item_pos = sb("item_pos", [P, NT, ITEMS + 1])
        item_gate = sb("item_gate", [P, NT, ITEMS + 1])
        cur = sb("cur", [P, 2, NT])
        plan = sb("plan", [1, 8], I32)
        assert plan_top[0] <= nc.sbuf_usable_end
        pt01 = sb("pt01", [P, 2, D], over="hs")
        rwords = sb("rwords", [P, RW], over="pt23")
        attn = sb("attn", [P, 2, C4], over="qT")
        ypT_hi = sb("ypT_hi", [P, 4, S], F32R, over="kT")
        yaT_hi = sb("yaT_hi", [P, 4, S], F32R, over="prob")
        yaT_lo = sb("yaT_lo", [P, 4, S], F32R, over="prob", skip=4 * 4 * S)
        dhid_hi = sb("dhid_hi", [P, 4, S], F32R, over="qT")
        dhid_lo = sb("dhid_lo", [P, 4, S], F32R, over="kT")
        dsilu = sb("dsilu", [P, 2, C4], over="vv")
        facc = sb("facc", [P, NT, D], over="bias")
        ynat = sb("ynat", [P, D], over="bias", skip=8 * D)
        xnat = sb("xnat", [P, D], over="bias", skip=12 * D)
        xT_hi = sb("xT_hi", [P, DT, CAP], F32R, over="prob")
        xT_lo = sb("xT_lo", [P, DT, CAP], F32R, over="prob", skip=4 * DT * CAP)
        ehid = sb("ehid", [P, C4], over="vv")
        eT_hi = sb("eT_hi", [P, 2, 4, CAP], F32R, over="pt23")
        eT_lo = sb("eT_lo", [P, 2, 4, CAP], F32R, over="pt23", skip=8 * 4 * CAP)
        pick = sb("pick", [P, NT, CAP], over="uT")
        gpick = sb("gpick", [P, NT, CAP], over="uT", skip=4 * NT * CAP)
        spread = sb("spread", [P, S], over="uT", skip=8 * NT * CAP)

        ident = cst[:, K_ID:K_ID + P]
        tri = cst[:, K_TRI:K_TRI + P]
        ones = cst[:, K_ONE:K_ONE + P]
        iota = cst[:, K_IOTA:K_IOTA + CAP]
        mask = cst[:, K_MASK:K_MASK + 2 * WIN].rearrange("p (b j) -> p b j", b=2)
        edge = cst[:, K_EDGE:K_EDGE + 64].rearrange("p (g s e) -> p g s e", g=4, s=2)
        before = cst[:, K_LT:K_LT + 64].rearrange("p (e f) -> p e f", e=NE)
        biasv = bias[:, :].rearrange("p (h b i j) -> p h b i j", h=HEADS, b=2, i=ROWS)

        def query_order(ap):
            v = ap.rearrange("p (r b c) -> p r b c", b=2, r=ROWS)
            a = [list(d) for d in v.ap]
            return bass.AP(v.tensor, v.offset + QC - 1, a[:-1] + [[-1, QC]])

        def token_order(ap):
            v = ap.rearrange("p (n c) -> p n c", c=QC)
            a = [list(d) for d in v.ap]
            return bass.AP(v.tensor, v.offset + QC - 1, a[:-1] + [[-1, QC]])

        def pt(k):
            t = pt01 if k < 2 else pt23
            return t[:, k % 2, :].rearrange("p (k m q) -> p k m q", k=2, m=4)

        def columns_half(ap, c):
            return ap.rearrange("p (t n) -> p t n", t=DT)[:, :, c * C2:(c + 1) * C2]

        def halves(seq, rows_first):
            out_ = []
            for c in range(2):
                n = 2 * seq + c
                src = ring[:, seq % RING, :]
                hi, lo = w_hi[:, n % STAGE, :], w_lo[:, n % STAGE, :]
                if rows_first:
                    out_.append((src[:, c * 8 * C2:(c + 1) * 8 * C2], hi, lo))
                else:
                    out_.append((columns_half(src, c), hi.rearrange("p (t n) -> p t n", t=DT),
                                 lo.rearrange("p (t n) -> p t n", t=DT)))
            return out_

        def rows_first(seq):
            j = seq % (MIX_LOADS + DENSE_LOADS)
            return 4 <= j < MIX_LOADS or (j >= MIX_LOADS and DENSE[j - MIX_LOADS][0] == "down")

        pa, pb, pc, pd = (ctx.enter_context(nc.psum_tensor(n, [P, 2 * C4], F32)) for n in ("pa", "pb", "pc", "pd"))

        w_landed = [sem(f"w_landed{i}") for i in range(RING)]
        hi_ready = sem("hi_ready")
        split_ready = sem("split_ready")
        half_done = sem("half_done")
        cst_landed = sem("cst_landed")
        x_landed = sem("x_landed")
        rows_landed = sem("rows_landed")
        poolw_landed = sem("poolw_landed")
        gpre_landed = sem("gpre_landed")
        gpost_landed = sem("gpost_landed")
        router_landed = sem("router_landed")
        rwords_landed = sem("rwords_landed")
        bias_part = sem("bias_part")
        cols_tp = sem("cols_tp")
        cols_ready = sem("cols_ready")
        squares = sem("squares")
        rms_pre = sem("rms_pre")
        hs_ready = sem("hs_ready")
        hs_tp = sem("hs_tp")
        hT_hi_ready = sem("hT_hi_ready")
        hT_ready = sem("hT_ready")
        fill_act = sem("fill_act")
        fill_dve = sem("fill_dve")
        qk_done = sem("qk_done")
        scored = sem("scored")
        negmax_ready = sem("negmax_ready")
        exp_done = sem("exp_done")
        tp0_done = sem("tp0_done")
        tp1_done = sem("tp1_done")
        pt_dve = sem("pt_dve")
        pt_act = sem("pt_act")
        pv_done = sem("pv_done")
        attn_ready = sem("attn_ready")
        pool_step = sem("pool_step")
        delta_ready = sem("delta_ready")
        pmix_done = sem("pmix_done")
        ypT_hi_ready = sem("ypT_hi_ready")
        ypT_ready = sem("ypT_ready")
        at_done = sem("at_done")
        yaT_hi_ready = sem("yaT_hi_ready")
        yaT_ready = sem("yaT_ready")
        rms_post = sem("rms_post")
        h_ready = sem("h_ready")
        dve_step = sem("dve_step")
        dsilu_ready = sem("dsilu_ready")
        dprod_ready = sem("dprod_ready")
        dhid_hi_ready = sem("dhid_hi_ready")
        dhid_ready = sem("dhid_ready")
        logits_done = sem("logits_done")
        lshift_ready = sem("lshift_ready")
        lexp_done = sem("lexp_done")
        sel_ready = sem("sel_ready")
        count_done = sem("count_done")
        plan_ready = sem("plan_ready")
        cur_ready = sem("cur_ready")
        pick_ready = sem("pick_ready")
        gather_done = sem("gather_done")
        xnat_dve = sem("xnat_dve")
        xnat_act = sem("xnat_act")
        xT_tp = sem("xT_tp")
        xT_hi_ready = sem("xT_hi_ready")
        xT_ready = sem("xT_ready")
        spread_tp = sem("spread_tp")
        spread_ready = sem("spread_ready")
        esilu_ready = sem("esilu_ready")
        ehid_ready = sem("ehid_ready")
        eT_tp = sem("eT_tp")
        eT_hi_ready = sem("eT_hi_ready")
        eT_ready = sem("eT_ready")
        ynat_dve = sem("ynat_dve")
        ynat_act = sem("ynat_act")
        comb_done = sem("comb_done")
        facc_done = sem("facc_done")
        moe_done = sem("moe_done")
        out_landed = sem("out_landed")

        MH = 2 * MOE0
        PH = 2 * PER_ITEM

        block = ctx.enter_context(nc.Block())

        @block.sync
        def _(sp):
            sp.dma_start(h[:, :, :], x[0].rearrange("(t p) n -> p t n", p=P)).then_inc(x_landed, 16)
            sp.dma_start(cst[:, :], consts).then_inc(cst_landed, 16)

            def load(seq, src, tiles):
                if seq >= RING:
                    sp.wait_ge(split_ready, 2 * (seq - RING) + 2)
                dst = ring[:, seq % RING, :].rearrange("p (t n) -> p t n", t=tiles)
                sp.dma_start(dst, src).then_inc(w_landed[seq % RING], 16)

            def by_tile(w):
                return w.rearrange("(t p) n -> p t n", p=P)

            for layer in range(DEPTH):
                s0 = mixing_first_load(layer)
                wi, wo = by_tile(w_in[layer]), by_tile(w_out[layer])
                for j, c in enumerate((1, 2, 3, 0)):
                    load(s0 + j, wi[:, :, c * C4:(c + 1) * C4], DT)
                for j in range(2):
                    load(s0 + 4 + j, wo[:, 4 * j:4 * j + 4, :], 4)
                if layer == 0:
                    for j, (what, b) in enumerate(DENSE):
                        cut = slice(b * C4, (b + 1) * C4)
                        if what == "down":
                            load(MIX_LOADS + j, by_tile(d_down[0, cut]), 4)
                        else:
                            w = d_gate if what == "gate" else d_up
                            load(MIX_LOADS + j, by_tile(w[0])[:, :, cut], DT)

            def load_item(i, expert):
                views = {n: w[0, bass.ds(expert, 1)].rearrange("e (t p) n -> p (e t) n", p=P)
                         for n, w in (("gate", e_gate), ("up", e_up), ("down", e_down))}
                for j, (what, b) in enumerate(EXPERT):
                    src = views[what]
                    src = src[:, 4 * b:4 * b + 4, :] if what == "down" else src[:, :, b * C4:(b + 1) * C4]
                    n = 4 if what == "down" else DT
                    sp.wait_ge(split_ready, i * PH + MH + 2 * (j - RING) + 2)
                    sp.dma_start(ring[:, (MOE0 + j) % RING, :].rearrange("p (t n) -> p t n", t=n), src).then_inc(
                        w_landed[(MOE0 + j) % RING], 16)

            with sp.Fori(0, NE) as e:
                load_item(e, e)
            sp.wait_ge(plan_ready, 1)
            extra = sp.value_load(plan[0:1, 7:8], min_val=0, max_val=EXTRA)
            with sp.Fori(0, EXTRA) as n:
                with sp.If(n < extra):
                    expert = sp.value_load(plan[0:1, bass.ds(n, 1)], min_val=0, max_val=NE - 1)
                    load_item(n + NE, expert)
            for t in range(NT):
                sp.wait_ge(h_ready, 2 * 3 + t + 1)
                sp.dma_start(out[0, t * P:(t + 1) * P, :], h[:, t, :]).then_inc(out_landed, 16)
            sp.wait_ge(out_landed, 16 * NT)

        @block.gpsimd
        def _(pool):
            steps = [0]

            def link(ins):
                steps[0] += 1
                ins.then_inc(pool_step, 1)
                pool.wait_ge(pool_step, steps[0])

            def load_gpre(n):
                src = (mix_pre if n % 2 == 0 else ffn_pre)[n // 2]
                if n:
                    pool.wait_ge(hs_ready, 2 * n)
                pool.dma_start(gpre[:, :], src.partition_broadcast(P)).then_inc(gpre_landed, 16)

            def load_gpost(n):
                src = (mix_post if n % 2 == 0 else ffn_post)[n // 2]
                if n:
                    pool.wait_ge(h_ready, 2 * n)
                pool.dma_start(gpost[:, :], src.partition_broadcast(P)).then_inc(gpost_landed, 16)

            def build_bias(layer):
                for quarter in range(4):
                    n = 4 * layer + quarter
                    first = layer * HEADS * RPB_H + 4 * quarter * RPB_H + 7 * RPB_R + RPB_R // 2 - 8
                    for r in range(ROWS):
                        src = bass.AP(rpb.tensor, first - RPB_R * r - (QC - 1), [[1, QC], [1, RW]])
                        pool.dma_start(rwords[QC * r:QC * (r + 1), :], src).then_inc(rwords_landed, 16)
                    pool.wait_ge(rwords_landed, 64 * (n + 1))
                    for b in range(2):
                        at = rwords[:, 8 - 8 * b:]
                        words = bass.AP(at.tensor, at.offset,
                                        [list(at.ap[0]), [RPB_H, 4], [RPB_R, ROWS], [1, WIN]])
                        m = mask[:, b, :].unsqueeze(1).unsqueeze(1).broadcast_to([P, 4, ROWS, WIN])
                        pool.tensor_tensor(biasv[:, 4 * quarter:4 * quarter + 4, b], words, m, ALU.add).then_inc(
                            bias_part, 1)
                    pool.wait_ge(bias_part, 2 * (n + 1))

            def window_means(layer):
                pool.wait_ge(fill_act, 4 * layer + 4)
                pool.wait_ge(fill_dve, 4 * layer + 4)
                for g in range(4):
                    w = 2 << g
                    src, n = uT[:, g, :], S + 2 * POOL_PAD
                    for k in range(g + 1):
                        n -= 1 << k
                        dst = (win_a, win_b)[k % 2]
                        link(pool.tensor_tensor(dst[:, 0:n], src[:, 0:n], src[:, (1 << k):(1 << k) + n], ALU.add))
                        src = dst
                    at = POOL_PAD - w // 2
                    mean = src[:, at:at + S]
                    link(pool.tensor_scalar(mean, mean, 1.0 / w, None, ALU.mult))
                    ends = bass.AP(src, mean.offset, [list(mean.ap[0]), [S - 8, 2], [1, 8]])
                    link(pool.tensor_tensor(ends, ends, edge[:, g], ALU.mult))
                    pool.tensor_tensor(delta[:, g, :], mean, uT[:, g, POOL_PAD:POOL_PAD + S],
                                       ALU.subtract).then_inc(delta_ready, 1)
                    pool.wait_ge(delta_ready, 4 * layer + g + 1)

            load_gpre(0)
            pool.dma_start(rows[:, :], pool_scale.rearrange("l (t p) -> (l t) p", p=P)).then_inc(rows_landed, 16)
            link(pool.memset(uT[:, :, :], 0.0))
            for layer in range(DEPTH):
                if layer:
                    pool.wait_ge(pmix_done, 2 * layer)
                pool.dma_start(poolw[:, :, :], pool_w[layer].rearrange("g c d -> c g d")).then_inc(poolw_landed, 16)
                if layer == 0:
                    pool.wait_ge(cst_landed, 16)
                    build_bias(0)
                    load_gpost(0)
                    load_gpre(1)
                    pool.dma_start(router_sb[:, :, :], router[0].rearrange("(t p) e -> p t e", p=P)).then_inc(
                        router_landed, 16)
                window_means(layer)
                load_gpost(2 * layer + 1)
                if layer == 0:
                    load_gpre(2)
                    build_bias(1)
                    load_gpost(2)
                    load_gpre(3)
            pool.wait_ge(scored, GROUPS * DEPTH)
            pool.wait_ge(pmix_done, 2 * DEPTH)
            pool.memset(spread[:, :], 0.0)
            pool.memset(ynat[:, C4:2 * C4], 0.0).then_inc(ynat_act, 1)
            pool.memset(ynat[:, 0:C4], 0.0).then_inc(ynat_dve, 1)
            pool.memset(facc[:, :, :].rearrange("p t n -> p (t n)"), 0.0).then_inc(facc_done, 4)

        @block.tensor
        def _(pe):
            mm = pe.matmul

            def product(dst, still, moving, start, stop):
                mm(dst, still[0], moving[0], start=start, stop=False)
                mm(dst, still[0], moving[1], start=False, stop=False)
                return mm(dst, still[1], moving[0], start=False, stop=stop)

            def split_half(n, item=None):
                pe.wait_ge(split_ready, n + 1 if item is None else item * PH + n + 1)
                return w_hi[:, n % STAGE, :], w_lo[:, n % STAGE, :]

            def transposes(n):
                for t in range(NT):
                    pe.wait_ge(hs_ready, 2 * n + t + 1)
                    bank = (pc, pd)[t]
                    for dt in range(DT):
                        ins = pe.transpose(bank[:, dt * P:(dt + 1) * P], hs[:, t, dt * P:(dt + 1) * P], ident)
                        if dt % 4 == 3:
                            ins.then_inc(hs_tp, 1)
                pe.wait_ge(hT_ready, 4 * (n + 1))

            def mixing(layer):
                h0 = 2 * mixing_first_load(layer)

                def fill(f, part):
                    if part == 0 and f >= 2:
                        pe.wait_ge((fill_act, fill_dve)[f % 2], 4 * layer + f // 2)
                    parts = [w.rearrange("p (t n) -> p t n", t=DT) for w in split_half(h0 + f)]
                    dst = pc[:, (f % 2) * C4 + part * C2:(f % 2) * C4 + (part + 1) * C2]
                    for dt in range(DT):
                        tok = (hT_hi[:, dt, :], hT_lo[:, dt, :])
                        if f in (4, 5):
                            still = [a[:, part * P:(part + 1) * P] for a in tok]
                            moving = [w[:, dt, :] for w in parts]
                        else:
                            still = [w[:, dt, part * P:(part + 1) * P] for w in parts]
                            moving = tok
                        ins = product(dst, still, moving, dt == 0, dt == DT - 1)
                    if part == 1:
                        ins.then_inc(half_done, 1)

                def scores(g):
                    b, rho = g // 4, g % 4
                    if g == 0:
                        pe.wait_ge(fill_act, 4 * layer + 2)
                        pe.wait_ge(fill_dve, 4 * layer + 2)
                    else:
                        pe.wait_ge(scored, GROUPS * layer + g)
                    rows32 = slice(HD * rho, HD * (rho + 1))
                    for m in range(4):
                        q = qT[rows32, m, b * P:(b + 1) * P]
                        k = kT[rows32, m, :].rearrange("p (r c) -> p r c", r=ROWS)[:, :, WIN0 * b:WIN0 * b + WIN]
                        ins = mm(pa[:, m * 256:m * 256 + ROWS * WIN], q, k, start=True, stop=True)
                    ins.then_inc(qk_done, 1)

                def turn(g):
                    pe.wait_ge(exp_done, GROUPS * layer + g + 1)
                    if g or layer:
                        pe.wait_ge(pt_dve, GROUPS * layer + g)
                        pe.wait_ge(pt_act, GROUPS * layer + g)
                    for kt in range(2):
                        for m in range(4):
                            ins = pe.transpose(pb[:, kt * C4 + m * P:kt * C4 + (m + 1) * P],
                                               prob[:, g % 2, m, 2 * kt:2 * kt + 2, :].rearrange("p i j -> p (i j)"),
                                               ident)
                        ins.then_inc((tp0_done, tp1_done)[kt], 1)

                def values(g):
                    b, rho = g // 4, g % 4
                    pe.wait_ge(pt_dve, GROUPS * layer + g + 1)
                    pe.wait_ge(pt_act, GROUPS * layer + g + 1)
                    if g == 0:
                        pe.wait_ge(fill_act, 4 * layer + 3)
                        pe.wait_ge(fill_dve, 4 * layer + 3)
                    for m in range(4):
                        c = (4 * m + rho) * HD
                        for kt in range(2):
                            ins = mm(pd[:, b * C4 + c:b * C4 + c + HD], pt(g % 4)[:, kt, m, :], vv[:, kt, c:c + HD],
                                     start=kt == 0, stop=kt == 1)
                    ins.then_inc(pv_done, 1)

                def project(half, src_hi, src_lo):
                    parts = [w.rearrange("p (t n) -> p t n", t=2) for w in split_half(h0 + 8 + half)]
                    for et in range(2):
                        e = 2 * (half % 2) + et
                        for t in range(NT):
                            still = [a[:, e, t * P:(t + 1) * P] for a in (src_hi, src_lo)]
                            for j in range(2):
                                ins = product((pa, pb)[t][:, j * C4:(j + 1) * C4], still,
                                              [w[:, et, j * C4:(j + 1) * C4] for w in parts],
                                              half == 0 and et == 0, half == 3 and et == 1)
                    ins.then_inc(half_done, 1)

                for f in range(4):
                    fill(f, 0)
                    fill(f, 1)
                for g in range(GROUPS):
                    scores(g)
                    if g:
                        turn(g - 1)
                    fill(4 + g // 2, g % 2)
                    if g == 4:
                        values(0)
                        values(1)
                    elif g == 5:
                        values(2)
                        values(3)
                    elif g > 5:
                        values(g - 2)
                turn(7)
                pe.wait_ge(poolw_landed, 16 * (layer + 1))
                pe.wait_ge(fill_act, 4 * layer + 4)
                pe.wait_ge(fill_dve, 4 * layer + 4)
                for g in range(4):
                    pe.wait_ge(delta_ready, 4 * layer + g + 1)
                    ins = mm(pc[:, g * S:(g + 1) * S], poolw[:, g, :], delta[:, g, :], start=True, stop=True)
                    if g % 2:
                        ins.then_inc(pmix_done, 1)
                values(6)
                values(7)
                pe.wait_ge(ypT_ready, layer + 1)
                project(0, ypT_hi, ypT_lo)
                project(1, ypT_hi, ypT_lo)
                for b in range(2):
                    pe.wait_ge(attn_ready, 2 * layer + b + 1)
                    for et in range(4):
                        ins = pe.transpose(pc[:, b * C4 + et * P:b * C4 + (et + 1) * P],
                                           attn[:, b, et * P:(et + 1) * P], ident)
                    ins.then_inc(at_done, 1)
                pe.wait_ge(yaT_ready, 2 * (layer + 1))
                project(2, yaT_hi, yaT_lo)
                project(3, yaT_hi, yaT_lo)

            def dense():
                h0 = 2 * MIX_LOADS
                for j, (what, b) in enumerate(DENSE):
                    for c in range(2):
                        parts = split_half(h0 + 2 * j + c)
                        if what == "down":
                            parts = [w.rearrange("p (t n) -> p t n", t=2) for w in parts]
                            pe.wait_ge(dhid_ready, 2 * b + c + 1)
                            for f in range(2):
                                for t in range(NT):
                                    still = [a[:, 2 * c + f, t * P:(t + 1) * P] for a in (dhid_hi, dhid_lo)]
                                    for n in range(2):
                                        ins = product((pa, pb)[t][:, n * C4:(n + 1) * C4], still,
                                                      [w[:, f, n * C4:(n + 1) * C4] for w in parts],
                                                      b == 0 and c == 0 and f == 0,
                                                      b == DBLOCKS - 1 and c == 1 and f == 1)
                        else:
                            parts = [w.rearrange("p (t n) -> p t n", t=DT) for w in parts]
                            if b:
                                pe.wait_ge(dsilu_ready if what == "gate" else dprod_ready, 2 * (b - 1) + c + 1)
                            bank = (pc if what == "gate" else pd)[:, c * C4:(c + 1) * C4]
                            for f in range(2):
                                for dt in range(DT):
                                    ins = product(bank[:, f * S:(f + 1) * S], [w[:, dt, f * P:(f + 1) * P] for w in parts],
                                                  (hT_hi[:, dt, :], hT_lo[:, dt, :]), dt == 0, dt == DT - 1)
                        ins.then_inc(half_done, 1)

            def routing():
                pe.wait_ge(router_landed, 16)
                for t in range(NT):
                    for dt in range(DT):
                        for part in (hT_hi, hT_lo):
                            ins = mm(pb[:, t * NE:(t + 1) * NE], part[:, dt, t * P:(t + 1) * P].bitcast(F32),
                                     router_sb[:, dt, :], start=dt == 0 and part is hT_hi,
                                     stop=dt == DT - 1 and part is hT_lo)
                ins.then_inc(logits_done, 1)
                pe.wait_ge(sel_ready, 1)
                sel = rt[:, 16:32].rearrange("p (t e) -> p t e", t=NT)
                mm(pb[:, C4:C4 + NE], tri, sel[:, 0], start=True, stop=True)
                mm(pb[:, C4 + NE:C4 + 2 * NE], ones, sel[:, 0], start=True, stop=False)
                mm(pb[:, C4 + NE:C4 + 2 * NE], tri, sel[:, 1], start=False, stop=True)
                mm(pb[:, C4 + 2 * NE:C4 + 3 * NE], ones, sel[:, 0], start=True, stop=False)
                mm(pb[:, C4 + 2 * NE:C4 + 3 * NE], ones, sel[:, 1], start=False, stop=True).then_inc(count_done, 1)

            def gather(i):
                pe.wait_ge(pick_ready, i + 1)
                pe.wait_ge(facc_done, i * 4 + 4)
                for j in range(2):
                    for t in range(NT):
                        ins = mm(pa[0:CAP, j * C4:(j + 1) * C4], pick[:, t, :], hs[:, t, j * C4:(j + 1) * C4],
                                 start=t == 0, stop=t == NT - 1)
                ins.then_inc(gather_done, 1)

            def turn_tokens(i):
                pe.wait_ge(xnat_dve, i + 1)
                pe.wait_ge(xnat_act, i + 1)
                for dt in range(DT):
                    at = dt // 4 * C4 + dt % 4 * CAP
                    ins = pe.transpose(pa[:, at:at + CAP], xnat[0:CAP, dt * P:(dt + 1) * P], ident[0:CAP, 0:CAP])
                ins.then_inc(xT_tp, 1)

            def combine(i, t):
                if t == 0:
                    pe.wait_ge(ynat_dve, i + 1)
                    pe.wait_ge(ynat_act, i + 1)
                for j in range(2):
                    pe.wait_ge(facc_done, i * 4 + 4 + 2 * t + j - 1)
                    mm(pa[:, j * C4:(j + 1) * C4], spread[0:CAP, t * P:(t + 1) * P],
                       ynat[0:CAP, j * C4:(j + 1) * C4], start=True, stop=True).then_inc(comb_done, 1)

            def expert_pass(i):
                def turn_hidden(b):
                    pe.wait_ge(ehid_ready, i * EBLOCKS + b + 1)
                    if b:
                        pe.wait_ge(eT_ready, i * EBLOCKS + b)
                    for f in range(4):
                        ins = pe.transpose(pb[:, f * CAP:(f + 1) * CAP], ehid[0:CAP, f * P:(f + 1) * P],
                                           ident[0:CAP, 0:CAP])
                    ins.then_inc(eT_tp, 1)

                pe.wait_ge(xT_ready, i + 1)
                for j, (what, b) in enumerate(EXPERT):
                    for c in range(2):
                        parts = split_half(MH + 2 * j + c, i)
                        if what == "down":
                            parts = [w.rearrange("p (t n) -> p t n", t=2) for w in parts]
                            if c == 0:
                                pe.wait_ge(eT_ready, i * EBLOCKS + b + 1)
                            for f in range(2):
                                still = [a[:, b % 2, 2 * c + f, :] for a in (eT_hi, eT_lo)]
                                for n in range(2):
                                    ins = product(pd[0:CAP, n * C4:(n + 1) * C4], still,
                                                  [w[:, f, n * C4:(n + 1) * C4] for w in parts],
                                                  b == 0 and c == 0 and f == 0,
                                                  b == EBLOCKS - 1 and c == 1 and f == 1)
                        else:
                            parts = [w.rearrange("p (t n) -> p t n", t=DT) for w in parts]
                            if b and c == 0:
                                pe.wait_ge(esilu_ready if what == "gate" else ehid_ready, i * EBLOCKS + b)
                            at = (0 if what == "gate" else C4) + c * C2
                            for dt in range(DT):
                                ins = product(pc[0:CAP, at:at + C2], (xT_hi[:, dt, :], xT_lo[:, dt, :]),
                                              [w[:, dt, :] for w in parts], dt == 0, dt == DT - 1)
                        ins.then_inc(half_done, 1)
                        if what == "gate" and b and c == 0:
                            turn_hidden(b - 1)
                        if (what, b, c) == ("down", EBLOCKS - 2, 0):
                            turn_hidden(EBLOCKS - 1)
                        if (what, b, c) == ("gate", 0, 1):
                            combine(i, 0)
                        if (what, b, c) == ("up", 0, 0):
                            combine(i, 1)
                    if (what, b) == ("up", 0):
                        for t in range(NT):
                            ins = pe.transpose(pb[0:CAP, C4 + t * P:C4 + (t + 1) * P], gpick[:, t, :], ident)
                        ins.then_inc(spread_tp, 1)
                    if (what, b) == ("down", 2):
                        gather(i + 1)
                    if (what, b) == ("down", 3):
                        turn_tokens(i + 1)

            pe.wait_ge(cst_landed, 16)
            pe.wait_ge(rows_landed, 16)
            pe.transpose(pa[:, 0:8], rows[:, :], ident[0:8, 0:8]).then_inc(cols_tp, 1)
            transposes(0)
            mixing(0)
            transposes(1)
            dense()
            transposes(2)
            mixing(1)
            transposes(3)
            routing()
            gather(0)
            turn_tokens(0)
            with pe.Fori(0, NE) as i:
                expert_pass(i)
            extra = pe.value_load(plan[0:1, 7:8], min_val=0, max_val=EXTRA)
            with pe.Fori(0, EXTRA) as n:
                with pe.If(n < extra):
                    expert_pass(n + NE)
            for t in range(NT):
                combine(extra + NE, t)

        @block.scalar
        def _(act):
            counts = {"split": 0, "squares": 0}

            def split_to(n):
                while counts["split"] < n:
                    k = counts["split"]
                    seq, c = k // 2, k % 2
                    if c == 0:
                        act.wait_ge(w_landed[seq % RING], 16 * (seq // RING + 1))
                    if k >= STAGE:
                        act.wait_ge(half_done, k - STAGE + 1)
                    src, hi, _ = halves(seq, rows_first(seq))[c]
                    act.activation(hi, src, ACT.Copy).then_inc(hi_ready, 1)
                    counts["split"] += 1

            def rms(dst, src, c):
                counts["squares"] += 1
                s = st[:, c:c + 1]
                act.activation(dst, src, ACT.Square, accum_out=s).then_inc(squares, 1)
                act.wait_ge(squares, counts["squares"])
                return act.activation(s, s, ACT.Sqrt, scale=1.0 / D, bias=cst[:, K_EPS:K_EPS + 1])

            def pre_norm(n):
                for t in range(NT):
                    if n == 0:
                        act.wait_ge(x_landed, 16)
                    else:
                        act.wait_ge(h_ready, 2 * (n - 1) + t + 1)
                    rms(hs[:, t, :], h[:, t, :], 2 * n + t).then_inc(rms_pre, 1)
                for t in range(NT):
                    for k in range(2):
                        act.wait_ge(hs_tp, 4 * n + 2 * t + k + 1)
                        act.activation(hT_hi[:, 4 * k:4 * k + 4, t * P:(t + 1) * P],
                                       (pc, pd)[t][:, k * C4:(k + 1) * C4].rearrange("p (a n) -> p a n", a=4),
                                       ACT.Copy).then_inc(hT_hi_ready, 1)

            def post_norm(n, done, value):
                for t in range(NT):
                    if t == 0:
                        act.wait_ge(done, value)
                    src = facc[:, t, :] if n == 3 else (pa, pb)[t][:, :]
                    rms(hs[:, t, :], src, 8 + 2 * n + t).then_inc(rms_post, 1)

            def mixing(layer):
                h0 = 2 * mixing_first_load(layer)

                def fill_q():
                    act.wait_ge(half_done, h0 + 1)
                    for m in range(2):
                        dst = qT[:, m, :].rearrange("p (b r c) -> p r b c", b=2, r=ROWS)
                        ins = act.activation(dst, query_order(pc[:, m * S:(m + 1) * S]), ACT.Copy, scale=HD ** -0.5)
                    ins.then_inc(fill_act, 1)

                def fill(f, dst):
                    act.wait_ge(half_done, h0 + f + 1)
                    act.activation(dst, pc[:, 0:C4].rearrange("p (a n) -> p a n", a=2), ACT.Copy).then_inc(fill_act, 1)

                def exps(g):
                    b, rho = g // 4, g % 4
                    act.wait_ge(negmax_ready, GROUPS * layer + g + 1)
                    for m in range(4):
                        p = prob[:, g % 2, m, :, WIN0 * b:WIN0 * b + WIN]
                        hd = 4 * m + rho
                        ins = act.activation(p, p, ACT.Exp, bias=negmax[:, g % 2, m:m + 1],
                                             accum_out=sums[:, b, hd:hd + 1])
                    ins.then_inc(exp_done, 1)

                def probs_out(g):
                    act.wait_ge(tp1_done, GROUPS * layer + g + 1)
                    if g >= 4:
                        act.wait_ge(pv_done, GROUPS * layer + g - 3)
                    act.activation(pt(g % 4)[:, 1], pb[:, C4:2 * C4].rearrange("p (m q) -> p m q", m=4),
                                   ACT.Copy).then_inc(pt_act, 1)

                split_to(h0 + 3)
                fill_q()
                split_to(h0 + 5)
                fill(2, kT[:, 0:2, :])
                split_to(h0 + 6)
                for g in range(GROUPS):
                    exps(g)
                    if g:
                        probs_out(g - 1)
                    if g == 1:
                        fill(4, vv[:, :, 0:C2])
                    if g == 5:
                        fill(6, uT[:, 0:2, POOL_PAD:POOL_PAD + S])
                    if g % 2:
                        split_to(h0 + 7 + g // 2)
                probs_out(7)
                act.wait_ge(pmix_done, 2 * layer + 2)
                for g in range(4):
                    c = 4 * layer + g
                    ins = act.activation(ypT_hi[:, g, :], pc[:, g * S:(g + 1) * S], ACT.Copy, scale=cols[:, c:c + 1])
                ins.then_inc(ypT_hi_ready, 1)
                split_to(h0 + 11)
                for b in range(2):
                    act.wait_ge(at_done, 2 * layer + b + 1)
                    dst = yaT_hi[:, :, :].rearrange("p e (r c) -> p (e r) c", r=ROWS)[:, :, QC * b:QC * (b + 1)]
                    act.activation(dst, token_order(pc[:, b * C4:(b + 1) * C4]), ACT.Copy).then_inc(yaT_hi_ready, 1)
                split_to(h0 + 14 if layer == 0 else h0 + 12)

            def dense():
                h0 = 2 * MIX_LOADS
                for j, (what, b) in enumerate(DENSE):
                    for c in range(2):
                        k = h0 + 2 * j + c
                        split_to(k + 3)
                        if what == "gate":
                            act.wait_ge(half_done, k + 1)
                            if b:
                                act.wait_ge(dhid_ready, 2 * (b - 1) + c + 1)
                            act.activation(dsilu[:, c, :], pc[:, c * C4:(c + 1) * C4], ACT.Silu).then_inc(
                                dsilu_ready, 1)
                        elif what == "up":
                            act.wait_ge(dprod_ready, 2 * b + c + 1)
                            act.activation(dhid_hi[:, 2 * c:2 * c + 2, :],
                                           dsilu[:, c, :].rearrange("p (f n) -> p f n", f=2), ACT.Copy).then_inc(
                                dhid_hi_ready, 1)

            def expert_split(i, k):
                seq, c = MOE0 + k // 2, k % 2
                if c == 0:
                    act.wait_ge(w_landed[seq % RING], i * (16 * PER_ITEM // RING) + 16 * (seq // RING + 1))
                act.wait_ge(half_done, i * PH + MH + k - STAGE + 1)
                src, hi, _ = halves(seq, EXPERT[k // 2][0] == "down")[c]
                act.activation(hi, src, ACT.Copy).then_inc(hi_ready, 1)

            def tokens_in(i):
                act.wait_ge(half_done, i * PH + MH - 4)
                act.wait_ge(xT_tp, i + 1)
                act.activation(xT_hi[:, :, :].rearrange("p (b t) n -> p b (t n)", b=2),
                               pa[:, :].rearrange("p (b n) -> p b n", b=2)[:, :, 0:4 * CAP], ACT.Copy).then_inc(
                    xT_hi_ready, 1)

            def tokens_gathered(i):
                act.wait_ge(gather_done, i + 1)
                act.activation(xnat[0:CAP, C4:2 * C4], pa[0:CAP, C4:2 * C4], ACT.Copy).then_inc(xnat_act, 1)

            def expert_pass(i, first, last):
                ahead = [first]

                def split_until(k):
                    while ahead[0] < min(k, last):
                        if ahead[0] < PH:
                            expert_split(i, ahead[0])
                        else:
                            expert_split(i + 1, ahead[0] - PH)
                        ahead[0] += 1

                def hidden_turned(b):
                    act.wait_ge(eT_tp, i * EBLOCKS + b + 1)
                    act.activation(eT_hi[:, b % 2].rearrange("p f n -> p (f n)"), pb[:, 0:4 * CAP],
                                   ACT.Copy).then_inc(eT_hi_ready, 1)

                for j, (what, b) in enumerate(EXPERT):
                    for c in range(2):
                        k = 2 * j + c
                        split_until(k + 3)
                        if what == "gate" and c == 0 and b:
                            hidden_turned(b - 1)
                        if (what, b, c) == ("down", EBLOCKS - 2, 0):
                            hidden_turned(EBLOCKS - 1)
                        if what == "gate" and c == 1:
                            act.wait_ge(half_done, i * PH + MH + k + 1)
                            if b:
                                act.wait_ge(eT_tp, i * EBLOCKS + b)
                            act.activation(ehid[0:CAP, :], pc[0:CAP, 0:C4], ACT.Silu).then_inc(esilu_ready, 1)
                        if (what, b, c) == ("up", 0, 1):
                            act.wait_ge(spread_tp, i + 1)
                            act.activation(spread[0:CAP, :], pb[0:CAP, C4:C4 + S], ACT.Copy).then_inc(spread_ready, 1)
                        if (what, b, c) == ("down", 2, 1):
                            tokens_gathered(i + 1)
                        if (what, b, c) == ("up", EBLOCKS - 1, 1):
                            tokens_in(i + 1)
                act.wait_ge(half_done, i * PH + MH + PH)
                act.activation(ynat[0:CAP, C4:2 * C4], pd[0:CAP, C4:2 * C4], ACT.Copy).then_inc(ynat_act, 1)
                split_until(PH + 3)

            act.wait_ge(cst_landed, 16)
            pre_norm(0)
            mixing(0)
            post_norm(0, half_done, 2 * MIX_LOADS)
            pre_norm(1)
            dense()
            post_norm(1, half_done, 2 * (MIX_LOADS + DENSE_LOADS))
            pre_norm(2)
            mixing(1)
            post_norm(2, half_done, MH)
            pre_norm(3)
            act.wait_ge(lshift_ready, 1)
            act.activation(rt[:, 48:64], rt[:, 32:48], ACT.Exp).then_inc(lexp_done, 1)
            for k in range(3):
                expert_split(0, k)
            tokens_gathered(0)
            tokens_in(0)
            with act.Fori(0, NE - 1) as i:
                expert_pass(i, 3, PH + 3)
            expert_pass(NE - 1, 3, PH)
            act.wait_ge(plan_ready, 1)
            extra = act.value_load(plan[0:1, 7:8], min_val=0, max_val=EXTRA)
            with act.Fori(0, EXTRA) as n:
                with act.If(n < extra):
                    expert_pass(n + NE, 0, PH)
            post_norm(3, moe_done, 1)

        @block.vector
        def _(dve):
            counts = {"step": 0, "split": 0}

            def link(ins):
                counts["step"] += 1
                ins.then_inc(dve_step, 1)
                dve.wait_ge(dve_step, counts["step"])

            def split_to(n):
                while counts["split"] < n:
                    k = counts["split"]
                    dve.wait_ge(hi_ready, k + 1)
                    src, hi, lo = halves(k // 2, rows_first(k // 2))[k % 2]
                    dve.tensor_tensor(lo, src, hi.bitcast(F32), ALU.subtract).then_inc(split_ready, 1)
                    counts["split"] += 1

            def rms_inverse(c):
                link(dve.reciprocal(st[:, c:c + 1], st[:, c:c + 1]))

            def pre_norm(n):
                dve.wait_ge(gpre_landed, 16 * (n + 1))
                for t in range(NT):
                    dve.wait_ge(rms_pre, 2 * n + t + 1)
                    rms_inverse(2 * n + t)
                    dve.scalar_tensor_tensor(out=hs[:, t, :], in0=h[:, t, :], scalar=st[:, 2 * n + t:2 * n + t + 1],
                                             in1=gpre[:, :], op0=ALU.mult, op1=ALU.mult).then_inc(hs_ready, 1)
                if n == 0:
                    dve.wait_ge(cols_tp, 1)
                    dve.tensor_copy(cols[:, :], pa[:, 0:8]).then_inc(cols_ready, 1)
                for t in range(NT):
                    for k in range(2):
                        dve.wait_ge(hT_hi_ready, 4 * n + 2 * t + k + 1)
                        part = (slice(None), slice(4 * k, 4 * k + 4), slice(t * P, (t + 1) * P))
                        dve.tensor_tensor(hT_lo[part],
                                          (pc, pd)[t][:, k * C4:(k + 1) * C4].rearrange("p (a n) -> p a n", a=4),
                                          hT_hi[part].bitcast(F32), ALU.subtract).then_inc(hT_ready, 1)

            def post_norm(n):
                dve.wait_ge(gpost_landed, 16 * (n + 1))
                for t in range(NT):
                    dve.wait_ge(rms_post, 2 * n + t + 1)
                    rms_inverse(8 + 2 * n + t)
                    src = facc[:, t, :] if n == 3 else (pa, pb)[t][:, :]
                    link(dve.scalar_tensor_tensor(out=hs[:, t, :], in0=src, scalar=st[:, 8 + 2 * n + t:9 + 2 * n + t],
                                                  in1=gpost[:, :], op0=ALU.mult, op1=ALU.mult))
                    dve.tensor_tensor(h[:, t, :], h[:, t, :], hs[:, t, :], ALU.add).then_inc(h_ready, 1)

            def mixing(layer):
                h0 = 2 * mixing_first_load(layer)

                def fill_q():
                    dve.wait_ge(half_done, h0 + 2)
                    for m in range(2, 4):
                        dst = qT[:, m, :].rearrange("p (b r c) -> p r b c", b=2, r=ROWS)
                        ins = dve.tensor_scalar(dst, query_order(pc[:, m * S:(m + 1) * S]), HD ** -0.5, None, ALU.mult)
                    ins.then_inc(fill_dve, 1)

                def fill(f, dst):
                    dve.wait_ge(half_done, h0 + f + 1)
                    dve.tensor_copy(dst, pc[:, C4:2 * C4].rearrange("p (a n) -> p a n", a=2)).then_inc(fill_dve, 1)

                def add_bias(g):
                    b, rho = g // 4, g % 4
                    if g == 0:
                        dve.wait_ge(bias_part, 8 * (layer + 1))
                    if g >= 2:
                        dve.wait_ge(tp1_done, GROUPS * layer + g - 1)
                    if g % 4 < 2:
                        c = WIN if b == 0 else 0
                        dve.memset(prob[:, g % 2, :, :, c:c + COLS - WIN].rearrange("p m i j -> p (m i) j"), 0.0)
                    dve.wait_ge(qk_done, GROUPS * layer + g + 1)
                    win = prob[:, g % 2, :, :, WIN0 * b:WIN0 * b + WIN]
                    sc = pa[:, :].rearrange("p (m n) -> p m n", m=4)[:, :, 0:ROWS * WIN].rearrange(
                        "p m (i j) -> p m i j", i=ROWS)
                    bs = bias[:, :].rearrange("p (m r b i j) -> p m r b i j", m=4, r=4, b=2, i=ROWS)[:, :, rho, b]
                    dve.tensor_tensor(win, sc, bs, ALU.add).then_inc(scored, 1)
                    dve.wait_ge(scored, GROUPS * layer + g + 1)
                    nm = negmax[:, g % 2, :]
                    link(dve.tensor_reduce(nm, win, AX.XY, ALU.max))
                    dve.tensor_scalar(nm, nm, -1.0, None, ALU.mult).then_inc(negmax_ready, 1)

                def probs_out(g):
                    dve.wait_ge(tp0_done, GROUPS * layer + g + 1)
                    if g >= 4:
                        dve.wait_ge(pv_done, GROUPS * layer + g - 3)
                    dve.tensor_copy(pt(g % 4)[:, 0], pb[:, 0:C4].rearrange("p (m q) -> p m q", m=4)).then_inc(
                        pt_dve, 1)

                split_to(h0 + 4)
                fill_q()
                split_to(h0 + 6)
                fill(3, kT[:, 2:4, :])
                for g in range(GROUPS):
                    add_bias(g)
                    if g:
                        probs_out(g - 1)
                    if g == 3:
                        fill(5, vv[:, :, C2:C4])
                    if g == 7:
                        fill(7, uT[:, 2:4, POOL_PAD:POOL_PAD + S])
                    if g % 2:
                        split_to(h0 + 7 + g // 2)
                probs_out(7)
                dve.wait_ge(ypT_hi_ready, layer + 1)
                for g in range(4):
                    c = 4 * layer + g
                    ins = dve.scalar_tensor_tensor(out=ypT_lo[:, g, :], in0=pc[:, g * S:(g + 1) * S],
                                                   scalar=cols[:, c:c + 1], in1=ypT_hi[:, g, :].bitcast(F32),
                                                   op0=ALU.mult, op1=ALU.subtract)
                ins.then_inc(ypT_ready, 1)
                dve.wait_ge(exp_done, GROUPS * (layer + 1))
                link(dve.reciprocal(rinv[:, :, :].rearrange("p b h -> p (b h)"),
                                    sums[:, :, :].rearrange("p b h -> p (b h)")))
                for b in range(2):
                    dve.wait_ge(pv_done, GROUPS * layer + 4 * (b + 1))
                    dve.tensor_tensor(attn[:, b, :].rearrange("p (h d) -> p h d", h=HEADS),
                                      pd[:, b * C4:(b + 1) * C4].rearrange("p (h d) -> p h d", h=HEADS),
                                      rinv[:, b, :].unsqueeze(2).broadcast_to([P, HEADS, HD]),
                                      ALU.mult).then_inc(attn_ready, 1)
                split_to(h0 + 11)
                for b in range(2):
                    dve.wait_ge(yaT_hi_ready, 2 * layer + b + 1)
                    cut = [a[:, :, :].rearrange("p e (r c) -> p (e r) c", r=ROWS)[:, :, QC * b:QC * (b + 1)]
                           for a in (yaT_lo, yaT_hi)]
                    dve.tensor_tensor(cut[0], token_order(pc[:, b * C4:(b + 1) * C4]), cut[1].bitcast(F32),
                                      ALU.subtract).then_inc(yaT_ready, 1)
                split_to(h0 + 14 if layer == 0 else h0 + 12)

            def dense():
                h0 = 2 * MIX_LOADS
                for j, (what, b) in enumerate(DENSE):
                    for c in range(2):
                        k = h0 + 2 * j + c
                        split_to(k + 3)
                        if what == "up":
                            dve.wait_ge(half_done, k + 1)
                            dve.wait_ge(dsilu_ready, 2 * b + c + 1)
                            buf = dsilu[:, c, :]
                            dve.tensor_tensor(buf, buf, pd[:, c * C4:(c + 1) * C4], ALU.mult).then_inc(dprod_ready, 1)
                            dve.wait_ge(dhid_hi_ready, 2 * b + c + 1)
                            dve.tensor_tensor(dhid_lo[:, 2 * c:2 * c + 2, :], buf.rearrange("p (f n) -> p f n", f=2),
                                              dhid_hi[:, 2 * c:2 * c + 2, :].bitcast(F32), ALU.subtract).then_inc(
                                dhid_ready, 1)

            def routing():
                def f(c, n):
                    return rt[:, c:c + n]

                def te(ap):
                    return ap.rearrange("p (t e) -> p t e", t=NT)

                lg, sel, sh, ex = f(0, 16), f(16, 16), f(32, 16), f(48, 16)
                m1, den = f(64, 2), f(66, 2)
                gates = f(80, 16)
                pos = f(96, 16)
                cnt, extras, base, inc = f(112, 8), f(120, 8), f(128, 8), f(136, 8)
                rho, slots, item, tmp = f(144, 16), f(160, 16), f(176, 16), f(192, 16)
                row = f(208, 8)
                big = f(256, 128).rearrange("p (t e f) -> p t e f", t=NT, e=NE)
                big2 = f(384, 128).rearrange("p (t e f) -> p t e f", t=NT, e=NE)
                rank = f(224, 16)
                dve.wait_ge(logits_done, 1)
                link(dve.tensor_copy(lg, pb[:, 0:16]))
                other = te(lg).unsqueeze(2).broadcast_to([P, NT, NE, NE])
                own = te(lg).unsqueeze(3).broadcast_to([P, NT, NE, NE])
                lower = before.unsqueeze(1).broadcast_to([P, NT, NE, NE])
                dve.tensor_tensor(big, other, own, ALU.is_gt)
                link(dve.tensor_tensor(big2, other, own, ALU.is_equal))
                for t in range(NT):
                    ins = dve.tensor_tensor(big2[:, t], big2[:, t], before, ALU.mult)
                link(ins)
                link(dve.tensor_tensor(f(256, 128), f(256, 128), f(384, 128), ALU.add))
                dve.tensor_reduce(te(rank), big, AX.X, ALU.add)
                link(dve.tensor_reduce(m1, te(lg), AX.X, ALU.max))
                dve.tensor_scalar(sel, rank, 1.5, None, ALU.is_lt).then_inc(sel_ready, 1)
                dve.tensor_tensor(te(sh), te(lg), m1.unsqueeze(2).broadcast_to([P, NT, NE]),
                                  ALU.subtract).then_inc(lshift_ready, 1)
                dve.wait_ge(sel_ready, 1)
                dve.wait_ge(lexp_done, 1)
                link(dve.tensor_tensor(ex, ex, sel, ALU.mult))
                link(dve.tensor_reduce(den, te(ex), AX.X, ALU.add))
                link(dve.reciprocal(den, den))
                link(dve.tensor_tensor(te(gates), te(ex), den.unsqueeze(2).broadcast_to([P, NT, NE]), ALU.mult))
                dve.wait_ge(count_done, 1)
                dve.tensor_copy(cnt, pb[:, C4 + 16:C4 + 24])
                link(dve.scalar_tensor_tensor(out=pos, in0=pb[:, C4:C4 + 16], scalar=1.0, in1=sel,
                                              op0=ALU.add, op1=ALU.mult))
                link(dve.tensor_scalar(pos, pos, -1.0, None, ALU.add))
                dve.tensor_copy(item_pos[:, :, 0:NE], te(pos))
                link(dve.tensor_copy(item_gate[:, :, 0:NE], te(gates)))
                make_picks(0)
                link(dve.tensor_scalar(extras, cnt, CAP + 0.5, None, ALU.is_gt))
                link(dve.tensor_scalar(rho, pos, CAP - 0.5, None, ALU.is_gt))
                k = 2
                while k * CAP < S:
                    link(dve.scalar_tensor_tensor(out=extras, in0=cnt, scalar=k * CAP + 0.5, in1=extras,
                                                  op0=ALU.is_gt, op1=ALU.add))
                    link(dve.scalar_tensor_tensor(out=rho, in0=pos, scalar=k * CAP - 0.5, in1=rho,
                                                  op0=ALU.is_gt, op1=ALU.add))
                    k += 1
                link(dve.tensor_tensor(big[:, 0], before, extras.unsqueeze(1).broadcast_to([P, NE, NE]), ALU.mult))
                link(dve.tensor_reduce(base, big[:, 0], AX.X, ALU.add))
                link(dve.tensor_tensor(inc, base, extras, ALU.add))
                link(dve.scalar_tensor_tensor(out=slots, in0=rho, scalar=-float(CAP), in1=pos,
                                              op0=ALU.mult, op1=ALU.add))
                link(dve.tensor_scalar(slots, slots, 1.0, None, ALU.add))
                link(dve.tensor_tensor(te(item), te(rho), base.unsqueeze(1).broadcast_to([P, NT, NE]), ALU.add))
                link(dve.tensor_scalar(tmp, rho, 0.5, None, ALU.is_gt))
                link(dve.tensor_tensor(item, item, tmp, ALU.mult))
                for n in range(EXTRA):
                    link(dve.scalar_tensor_tensor(out=tmp, in0=item, scalar=float(n + 1), in1=slots,
                                                  op0=ALU.is_equal, op1=ALU.mult))
                    link(dve.tensor_reduce(item_pos[:, :, NE + n], te(tmp), AX.X, ALU.add))
                    link(dve.scalar_tensor_tensor(out=tmp, in0=item, scalar=float(n + 1), in1=gates,
                                                  op0=ALU.is_equal, op1=ALU.mult))
                    link(dve.tensor_reduce(item_gate[:, :, NE + n], te(tmp), AX.X, ALU.add))
                    link(dve.tensor_scalar(tmp[:, 0:NE], inc, n + 0.5, None, ALU.is_lt))
                    link(dve.tensor_reduce(row[:, n:n + 1], tmp[:, 0:NE], AX.X, ALU.add))
                link(dve.tensor_scalar(item_pos[:, :, NE:ITEMS], item_pos[:, :, NE:ITEMS], -1.0, None, ALU.add))
                link(dve.memset(row[:, EXTRA:7], 0.0)) if EXTRA < 7 else None
                link(dve.tensor_scalar(row[:, 0:7], row[:, 0:7], float(NE - 1), None, ALU.min))
                link(dve.tensor_copy(row[:, 7:8], inc[:, 7:8]))
                dve.tensor_copy(plan[0:1, :], row[0:1, :]).then_inc(plan_ready, 1)
                for a, pad in ((item_pos, -1.0), (item_gate, 0.0)):
                    link(dve.memset(a[:, :, ITEMS], pad))

            def expert_split(i, k):
                seq, c = MOE0 + k // 2, k % 2
                dve.wait_ge(hi_ready, i * PH + MH + k + 1)
                src, hi, lo = halves(seq, EXPERT[k // 2][0] == "down")[c]
                dve.tensor_tensor(lo, src, hi.bitcast(F32), ALU.subtract).then_inc(split_ready, 1)

            def make_picks(i):
                at = bass.ds(i, 1)
                dve.tensor_copy(cur[:, 0, :], item_pos[:, :, at].rearrange("p t i -> p (t i)"))
                dve.tensor_copy(cur[:, 1, :], item_gate[:, :, at].rearrange("p t i -> p (t i)")).then_inc(cur_ready, 1)
                dve.wait_ge(cur_ready, i + 1)
                for t in range(NT):
                    dve.tensor_scalar(pick[:, t, :], iota, cur[:, 0, t:t + 1], None, ALU.is_equal)
                    ins = dve.tensor_scalar(gpick[:, t, :], iota, cur[:, 0, t:t + 1], cur[:, 1, t:t + 1],
                                            ALU.is_equal, ALU.mult)
                ins.then_inc(pick_ready, 1)

            def tokens_gathered(i):
                dve.wait_ge(gather_done, i + 1)
                dve.tensor_copy(xnat[0:CAP, 0:C4], pa[0:CAP, 0:C4]).then_inc(xnat_dve, 1)

            def tokens_in(i):
                dve.wait_ge(xT_hi_ready, i + 1)
                dve.tensor_tensor(xT_lo[:, :, :].rearrange("p (b t) n -> p b (t n)", b=2),
                                  pa[:, :].rearrange("p (b n) -> p b n", b=2)[:, :, 0:4 * CAP],
                                  xT_hi[:, :, :].rearrange("p (b t) n -> p b (t n)", b=2).bitcast(F32),
                                  ALU.subtract).then_inc(xT_ready, 1)

            def combined(i, t):
                for j in range(2):
                    q = facc[:, t, j * C4:(j + 1) * C4]
                    dve.wait_ge(comb_done, i * 4 + 2 * t + j + 1)
                    dve.wait_ge(facc_done, i * 4 + 2 * t + j + 1)
                    dve.tensor_tensor(q, q, pa[:, j * C4:(j + 1) * C4], ALU.add).then_inc(facc_done, 1)

            def expert_pass(i, first, last):
                ahead = [first]

                def split_until(k):
                    while ahead[0] < min(k, last):
                        if ahead[0] < PH:
                            expert_split(i, ahead[0])
                        else:
                            expert_split(i + 1, ahead[0] - PH)
                        ahead[0] += 1

                def hidden_turned(b):
                    dve.wait_ge(eT_hi_ready, i * EBLOCKS + b + 1)
                    dve.tensor_tensor(eT_lo[:, b % 2].rearrange("p f n -> p (f n)"), pb[:, 0:4 * CAP],
                                      eT_hi[:, b % 2].rearrange("p f n -> p (f n)").bitcast(F32),
                                      ALU.subtract).then_inc(eT_ready, 1)

                for j, (what, b) in enumerate(EXPERT):
                    for c in range(2):
                        k = 2 * j + c
                        split_until(k + 3)
                        if what == "gate" and c == 0 and b:
                            hidden_turned(b - 1)
                        if (what, b, c) == ("down", EBLOCKS - 2, 0):
                            hidden_turned(EBLOCKS - 1)
                        if (what, b, c) == ("gate", 0, 1):
                            combined(i, 0)
                        if (what, b, c) == ("up", 0, 0):
                            combined(i, 1)
                        if what == "up" and c == 1:
                            dve.wait_ge(half_done, i * PH + MH + k + 1)
                            dve.wait_ge(esilu_ready, i * EBLOCKS + b + 1)
                            dve.tensor_tensor(ehid[0:CAP, :], ehid[0:CAP, :], pc[0:CAP, C4:2 * C4],
                                              ALU.mult).then_inc(ehid_ready, 1)
                            if b == 0:
                                dve.wait_ge(spread_tp, i + 1)
                                make_picks(i + 1)
                        if (what, b, c) == ("down", 2, 1):
                            tokens_gathered(i + 1)
                        if (what, b, c) == ("up", EBLOCKS - 1, 1):
                            tokens_in(i + 1)
                dve.wait_ge(half_done, i * PH + MH + PH)
                dve.tensor_copy(ynat[0:CAP, 0:C4], pd[0:CAP, 0:C4]).then_inc(ynat_dve, 1)
                split_until(PH + 3)

            pre_norm(0)
            mixing(0)
            post_norm(0)
            pre_norm(1)
            dense()
            post_norm(1)
            pre_norm(2)
            mixing(1)
            post_norm(2)
            pre_norm(3)
            routing()
            for k in range(3):
                expert_split(0, k)
            tokens_gathered(0)
            tokens_in(0)
            with dve.Fori(0, NE - 1) as i:
                expert_pass(i, 3, PH + 3)
            expert_pass(NE - 1, 3, PH)
            dve.wait_ge(plan_ready, 1)
            extra = dve.value_load(plan[0:1, 7:8], min_val=0, max_val=EXTRA)
            with dve.Fori(0, EXTRA) as n:
                with dve.If(n < extra):
                    expert_pass(n + NE, 0, PH)
            for t in range(NT):
                combined(extra + NE, t)
            dve.memset(st[:, 32:33], 0.0).then_inc(moe_done, 1)
            post_norm(3)


_INS = ['x', 'mix_norm_pre', 'mix_norm_post', 'ffn_norm_pre', 'ffn_norm_post', 'w_in', 'pool_w', 'pool_scale',
        'na_rpb', 'w_out', 'dense_w_gate', 'dense_w_up', 'dense_w_down', 'moe_router', 'moe_w_gate', 'moe_w_up',
        'moe_w_down']


def shape_constants():
    import numpy as np
    c = np.zeros((P, K_ALL), np.float32)
    p = np.arange(P)
    c[:, K_ID:K_ID + P] = np.eye(P)
    c[:, K_TRI:K_TRI + P] = p[:, None] < p[None, :]
    c[:, K_ONE:K_ONE + P] = 1
    c[:, K_IOTA:K_IOTA + CAP] = np.arange(CAP)
    for b in range(2):
        first = np.clip(QC - 1 - p % QC + QC * b - KWIN // 2, 0, COLS - KWIN)[:, None]
        col = WIN0 * b + np.arange(WIN)[None, :]
        seen = (col >= first) & (col < first + KWIN)
        c[:, K_MASK + b * WIN:K_MASK + (b + 1) * WIN] = np.where(seen, 0, MASKED)
    t = np.concatenate([np.arange(8), np.arange(S - 8, S)])
    for g in range(4):
        w = 2 << g
        n = np.clip(t + w - w // 2, 0, S) - np.clip(t - w // 2, 0, S)
        c[:, K_EDGE + 16 * g:K_EDGE + 16 * (g + 1)] = w / n
    e = np.arange(NE)
    c[:, K_EPS] = EPS
    c[:, K_LT:K_LT + 64] = (e[None, :] < e[:, None]).reshape(-1)
    return c


def kernel(**inputs):
    import numpy as np
    import concourse.bacc as bacc
    from concourse.bass_utils import run_bass_kernel_spmd

    nc = bacc.Bacc("TRN2", target_bir_lowering=False, num_devices=1)
    arrays, args = {}, []
    for name in _INS:
        a = np.ascontiguousarray(inputs[name])
        arrays[f"in_{name}"] = a
        args.append(nc.dram_tensor(f"in_{name}", a.shape, mybir.dt.from_np(a.dtype), kind="ExternalInput").ap())
    consts = shape_constants()
    arrays["in_consts"] = consts
    args.append(nc.dram_tensor("in_consts", consts.shape, F32, kind="ExternalInput").ap())
    args.append(nc.dram_tensor("out", (1, S, D), F32, kind="ExternalOutput").ap())
    hybrid_encoder(nc, *args)
    r = run_bass_kernel_spmd(nc, [arrays], core_ids=[0])
    return r.results[0]["out"]
```

```python
from contextlib import ExitStack

import concourse.bass as bass
from concourse import mybir
from concourse.alu_op_type import AluOpType as ALU

ACT = mybir.ActivationFunctionType
AX = mybir.AxisListType
F32 = mybir.dt.float32
F32R = mybir.dt.float32r
I32 = mybir.dt.int32

P = 128
D = 1024
DT = D // P
S = 256
NT = S // P
DEPTH = 2
C4 = 512
C2 = 256
HEADS = 16
HD = 32
ROWS, COLS = 4, 64
QC = 32
WIN = 40
WIN0 = 24
KWIN = 16
RPB_H, RPB_R = 15 * 31, 31
RW = 3 * RPB_H + 3 * RPB_R + (WIN - 1) + 8 + 1
MASKED = -1e30
EPS = 1e-6
POOL_PAD = 8
FE = 3584
DBLOCKS = 4096 // C4
EBLOCKS = FE // C4
NE = 8
CAP = 80
EXTRA = 2 * S // (CAP + 1)
ITEMS = NE + EXTRA
GROUPS = 8

RING = 3
SPARE_EVERY = 7
SPARE_AT = 3
STAGE = 3
MIX_LOADS = 6
DENSE_LOADS = 3 * DBLOCKS
PER_ITEM = 3 * EBLOCKS
MOE0 = 2 * MIX_LOADS + DENSE_LOADS
RING_ITEM = PER_ITEM - PER_ITEM // SPARE_EVERY
assert PER_ITEM % SPARE_EVERY == 0 and RING_ITEM % RING == 0 and MOE0 % RING == 0
assert 2 * PER_ITEM % STAGE == 0 and 2 * MOE0 % STAGE == 0


def ffn_order(blocks):
    order = [("gate", 0), ("up", 0)]
    for b in range(1, blocks):
        order += [("gate", b), ("down", b - 1), ("up", b)]
    return order + [("down", blocks - 1)]


DENSE = ffn_order(DBLOCKS)
EXPERT = ffn_order(EBLOCKS)
EXPERT[-3:] = [EXPERT[-2], EXPERT[-3], EXPERT[-1]]


def ring_number(j):
    return j - (j + SPARE_EVERY - 1 - SPARE_AT) // SPARE_EVERY


def slot_of(seq):
    if seq < MOE0:
        return seq % RING, seq // RING + 1
    j = seq - MOE0
    if j % SPARE_EVERY == SPARE_AT:
        return RING, j // SPARE_EVERY + 1
    n = ring_number(j)
    return n % RING, MOE0 // RING + n // RING + 1


def load_before(j):
    if j % SPARE_EVERY == SPARE_AT:
        return j - SPARE_EVERY
    n = ring_number(j) - RING
    return n + (n + SPARE_EVERY - 1 - SPARE_AT) // (SPARE_EVERY - 1)


def slot_loads(slot):
    return PER_ITEM // SPARE_EVERY if slot == RING else RING_ITEM // RING


K_ID, K_TRI, K_ONE = 0, P, 2 * P
K_IOTA = 3 * P
K_MASK = K_IOTA + CAP
K_EDGE = K_MASK + 2 * WIN
K_LT = K_EDGE + 64
K_EPS = K_LT + 64
K_ALL = K_EPS + 1


def mixing_first_load(layer):
    return layer * (MIX_LOADS + DENSE_LOADS)


def hybrid_encoder(nc, x, mix_pre, mix_post, ffn_pre, ffn_post, w_in, pool_w, pool_scale, rpb,
                   w_out, d_gate, d_up, d_down, router, e_gate, e_up, e_down, consts, out):
    with ExitStack() as ctx:
        def sem(name):
            return ctx.enter_context(nc.semaphore(name))

        plan_top = [-(-nc.sbuf_base // 32) * 32]

        def sb(name, shape, dt=F32, over=None, skip=0):
            size = 4
            for n in shape[1:]:
                size *= n
            if over is None:
                at = plan_top[0]
                plan_top[0] += -(-size // 32) * 32
            else:
                at = addr[over] + skip
            addr[name] = at
            return nc.alloc_sbuf_tensor_at(name, shape, dt, offset=at)

        addr = {}
        ring = sb("ring", [P, RING, 8 * C4])
        w_hi = sb("w_hi", [P, STAGE, 8 * C2], F32R)
        w_lo = sb("w_lo", [P, STAGE, 8 * C2], F32R)
        h = sb("h", [P, NT, D])
        hs = sb("hs", [P, NT, D])
        hT_hi = sb("hT_hi", [P, DT, S], F32R)
        hT_lo = sb("hT_lo", [P, DT, S], F32R)
        gpre = sb("gpre", [P, D])
        gpost = sb("gpost", [P, D])
        router_sb = sb("router_sb", [P, DT, NE])
        cst = sb("cst", [P, K_ALL])
        rows = sb("rows", [8, P])
        cols = sb("cols", [P, 8])
        st = sb("st", [P, 64])
        qT = sb("qT", [P, 4, S])
        kT = sb("kT", [P, 4, S])
        vv = sb("vv", [P, NT, C4])
        uT = sb("uT", [P, 4, S + 2 * POOL_PAD])
        win_a = sb("win_a", [P, S + 2 * POOL_PAD])
        win_b = sb("win_b", [P, S + 2 * POOL_PAD])
        bias = sb("bias", [P, HEADS * 2 * ROWS * WIN])
        prob = sb("prob", [P, 2, 4, ROWS, COLS])
        pt23 = sb("pt23", [P, 2, D])
        poolw = sb("poolw", [P, 4, P])
        ypT_lo = sb("ypT_lo", [P, 4, S], F32R)
        delta = sb("delta", [P, 4, S])
        negmax = sb("negmax", [P, 2, 4])
        sums = sb("sums", [P, 2, 4])
        rinv = sb("rinv", [P, 2, 4])
        router_hi = sb("router_hi", [P, DT, NE], F32R)
        router_lo = sb("router_lo", [P, DT, NE], F32R)
        rt = sb("rt", [P, 512])
        item_pos = sb("item_pos", [P, NT, ITEMS + 1])
        item_gate = sb("item_gate", [P, NT, ITEMS + 1])
        cur = sb("cur", [P, 2, NT])
        plan = sb("plan", [1, 8], I32)
        assert plan_top[0] <= nc.sbuf_usable_end
        pt01 = sb("pt01", [P, 2, D], over="hs")
        assert 4 * RW <= 4 * 2 * D
        rwords = (sb("rwords_a", [P, RW], over="pt23"),
                  sb("rwords_b", [P, RW], over="ypT_lo"))
        win_c = sb("win_c", [P, S + 2 * POOL_PAD], over="qT")
        win_d = sb("win_d", [P, S + 2 * POOL_PAD], over="qT", skip=2048)
        lgT = sb("lgT", [NE, S], over="win_a")
        ypT_hi = sb("ypT_hi", [P, 4, S], F32R, over="kT")
        yaT_hi = sb("yaT_hi", [P, 4, S], F32R, over="prob")
        yaT_lo = sb("yaT_lo", [P, 4, S], F32R, over="prob", skip=4 * 4 * S)
        dhid_hi = sb("dhid_hi", [P, 4, S], F32R, over="qT")
        dhid_lo = sb("dhid_lo", [P, 4, S], F32R, over="kT")
        dsilu = sb("dsilu", [P, 2, C4], over="vv")
        spare = sb("spare", [P, 8 * C4], over="bias")
        facc = sb("facc", [P, NT, D], over="qT")
        ynat = sb("ynat", [P, D], over="ypT_lo")
        xnat = sb("xnat", [P, D], over="delta")
        xT_hi = sb("xT_hi", [P, DT, CAP], F32R, over="prob")
        xT_lo = sb("xT_lo", [P, DT, CAP], F32R, over="prob", skip=4 * DT * CAP)
        ehid = sb("ehid", [P, C4], over="vv")
        eT_hi = sb("eT_hi", [P, 2, 4, CAP], F32R, over="pt23")
        eT_lo = sb("eT_lo", [P, 2, 4, CAP], F32R, over="pt23", skip=8 * 4 * CAP)
        hs_hi = sb("hs_hi", [P, NT, D], F32R, over="hT_hi")
        hs_lo = sb("hs_lo", [P, NT, D], F32R, over="hT_lo")
        pick = sb("pick", [P, NT, CAP], F32R, over="uT")
        gpick = sb("gpick", [P, NT, CAP], over="uT", skip=4 * NT * CAP)
        spread = sb("spread", [P, S], over="uT", skip=8 * NT * CAP)

        ident = cst[:, K_ID:K_ID + P]
        tri = cst[:, K_TRI:K_TRI + P]
        ones = cst[:, K_ONE:K_ONE + P]
        iota = cst[:, K_IOTA:K_IOTA + CAP]
        mask = cst[:, K_MASK:K_MASK + 2 * WIN].rearrange("p (b j) -> p b j", b=2)
        edge = cst[:, K_EDGE:K_EDGE + 64].rearrange("p (g s e) -> p g s e", g=4, s=2)
        before = cst[:, K_LT:K_LT + 64].rearrange("p (e f) -> p e f", e=NE)
        biasv = bias[:, :].rearrange("p (h b i j) -> p h b i j", h=HEADS, b=2, i=ROWS)

        def query_order(ap):
            v = ap.rearrange("p (r b c) -> p r b c", b=2, r=ROWS)
            a = [list(d) for d in v.ap]
            return bass.AP(v.tensor, v.offset + QC - 1, a[:-1] + [[-1, QC]])

        def token_order(ap):
            v = ap.rearrange("p (n c) -> p n c", c=QC)
            a = [list(d) for d in v.ap]
            return bass.AP(v.tensor, v.offset + QC - 1, a[:-1] + [[-1, QC]])

        def pt(k):
            t = pt01 if k < 2 else pt23
            return t[:, k % 2, :].rearrange("p (k m q) -> p k m q", k=2, m=4)

        def columns_half(ap, c):
            return ap.rearrange("p (t n) -> p t n", t=DT)[:, :, c * C2:(c + 1) * C2]

        def slot_buffer(slot):
            return spare[:, :] if slot == RING else ring[:, slot, :]

        def halves(seq, rows_first):
            out_ = []
            for c in range(2):
                n = 2 * seq + c
                src = slot_buffer(slot_of(seq)[0])
                hi, lo = w_hi[:, n % STAGE, :], w_lo[:, n % STAGE, :]
                if rows_first:
                    out_.append((src[:, c * 8 * C2:(c + 1) * 8 * C2], hi, lo))
                else:
                    out_.append((columns_half(src, c), hi.rearrange("p (t n) -> p t n", t=DT),
                                 lo.rearrange("p (t n) -> p t n", t=DT)))
            return out_

        def rows_first(seq):
            j = seq % (MIX_LOADS + DENSE_LOADS)
            return 4 <= j < MIX_LOADS or (j >= MIX_LOADS and DENSE[j - MIX_LOADS][0] == "down")

        pa, pb, pc, pd = (ctx.enter_context(nc.psum_tensor(n, [P, 2 * C4], F32)) for n in ("pa", "pb", "pc", "pd"))

        half_landed = sem("half_landed")
        w_landed = [sem(f"w_landed{i}") for i in range(RING + 1)]
        hi_ready = sem("hi_ready")
        split_ready = sem("split_ready")
        half_done = sem("half_done")
        cst_landed = sem("cst_landed")
        x_landed = sem("x_landed")
        rows_landed = sem("rows_landed")
        poolw_landed = sem("poolw_landed")
        gpre_landed = sem("gpre_landed")
        gpost_landed = sem("gpost_landed")
        router_landed = sem("router_landed")
        rwords_landed = [[sem(f"rwords_landed{layer}_{i}") for i in range(2)] for layer in range(DEPTH)]
        bias_part = sem("bias_part")
        cols_tp = sem("cols_tp")
        cols_ready = sem("cols_ready")
        squares = sem("squares")
        rms_pre = sem("rms_pre")
        hs_ready = sem("hs_ready")
        hs_tp = sem("hs_tp")
        hT_hi_ready = sem("hT_hi_ready")
        hT_ready = sem("hT_ready")
        fill_act = sem("fill_act")
        fill_dve = sem("fill_dve")
        qk_done = sem("qk_done")
        scored = sem("scored")
        negmax_ready = sem("negmax_ready")
        exp_done = sem("exp_done")
        prob_ready = sem("prob_ready")
        tp0_done = sem("tp0_done")
        tp1_done = sem("tp1_done")
        pt_dve = sem("pt_dve")
        pt_act = sem("pt_act")
        pv_done = sem("pv_done")
        pool_step = sem("pool_step")
        delta_ready = sem("delta_ready")
        delta_dve_ready = sem("delta_dve_ready")
        pmix_done = sem("pmix_done")
        ypT_hi_ready = sem("ypT_hi_ready")
        ypT_ready = sem("ypT_ready")
        yaT_hi_ready = sem("yaT_hi_ready")
        yaT_ready = sem("yaT_ready")
        rms_post = sem("rms_post")
        tile0_done = sem("tile0_done")
        h_ready = sem("h_ready")
        dve_step = sem("dve_step")
        dsilu_ready = sem("dsilu_ready")
        dprod_ready = sem("dprod_ready")
        dhid_hi_ready = sem("dhid_hi_ready")
        dhid_ready = sem("dhid_ready")
        router_hi_ready = sem("router_hi_ready")
        router_ready = sem("router_ready")
        logits_done = sem("logits_done")
        lgT_ready = sem("lgT_ready")
        logits_tp = sem("logits_tp")
        lshift_ready = sem("lshift_ready")
        lexp_done = sem("lexp_done")
        sel_ready = sem("sel_ready")
        count_done = sem("count_done")
        slots_ready = sem("slots_ready")
        plan_ready = sem("plan_ready")
        hs_hi_ready = sem("hs_hi_ready")
        hs_split = sem("hs_split")
        cur_ready = sem("cur_ready")
        pick_ready = sem("pick_ready")
        gather_done = sem("gather_done")
        xnat_dve = sem("xnat_dve")
        xnat_act = sem("xnat_act")
        xT_tp = sem("xT_tp")
        xT_hi_ready = sem("xT_hi_ready")
        xT_ready = sem("xT_ready")
        spread_tp = sem("spread_tp")
        spread_ready = sem("spread_ready")
        esilu_ready = sem("esilu_ready")
        ehid_ready = sem("ehid_ready")
        eT_tp = sem("eT_tp")
        eT_hi_ready = sem("eT_hi_ready")
        eT_ready = sem("eT_ready")
        ynat_dve = sem("ynat_dve")
        ynat_act = sem("ynat_act")
        comb_done = sem("comb_done")
        facc_done = sem("facc_done")
        out_landed = sem("out_landed")

        def load_rwords(eng, layer, quarter):
            n = 4 * layer + quarter
            first = layer * HEADS * RPB_H + 4 * quarter * RPB_H + 7 * RPB_R + RPB_R // 2 - 8
            if n >= 2:
                eng.wait_ge(bias_part, 2 * (n - 1))
            for r in range(ROWS):
                src = bass.AP(rpb.tensor, first - RPB_R * r - (QC - 1), [[1, QC], [1, RW]])
                eng.dma_start(rwords[n % 2][QC * r:QC * (r + 1), :], src).then_inc(
                    rwords_landed[layer][quarter % 2], 16)

        def window_delta(eng, link, layer, g, bufs):
            w = 2 << g
            src, n = uT[:, g, :], S + 2 * POOL_PAD
            for k in range(g + 1):
                n -= 1 << k
                dst = bufs[k % 2]
                link(eng.tensor_tensor(dst[:, 0:n], src[:, 0:n], src[:, (1 << k):(1 << k) + n], ALU.add))
                src = dst
            at = POOL_PAD - w // 2
            mean = src[:, at:at + S]
            link(eng.tensor_scalar(mean, mean, 1.0 / w, None, ALU.mult))
            ends = bass.AP(src, mean.offset, [list(mean.ap[0]), [S - 8, 2], [1, 8]])
            link(eng.tensor_tensor(ends, ends, edge[:, g], ALU.mult))
            return eng.tensor_tensor(delta[:, g, :], mean, uT[:, g, POOL_PAD:POOL_PAD + S], ALU.subtract)

        MH = 2 * MOE0
        PH = 2 * PER_ITEM

        block = ctx.enter_context(nc.Block())

        @block.sync
        def _(sp):
            sp.dma_start(h[:, :, :], x[0].rearrange("(t p) n -> p t n", p=P)).then_inc(x_landed, 16)
            sp.dma_start(cst[:, :], consts).then_inc(cst_landed, 16)

            def load(seq, src, tiles):
                if seq >= RING:
                    sp.wait_ge(split_ready, 2 * (seq - RING) + 2)
                dst = ring[:, seq % RING, :].rearrange("p (t n) -> p t n", t=tiles)
                if seq == 0:
                    sp.dma_start(dst[:, :, 0:C2], src[:, :, 0:C2]).then_inc(half_landed, 16)
                    dst, src = dst[:, :, C2:C4], src[:, :, C2:C4]
                sp.dma_start(dst, src).then_inc(w_landed[seq % RING], 16)

            def by_tile(w):
                return w.rearrange("(t p) n -> p t n", p=P)

            for layer in range(DEPTH):
                s0 = mixing_first_load(layer)
                wi, wo = by_tile(w_in[layer]), by_tile(w_out[layer])
                for j, c in enumerate((1, 2, 3, 0)):
                    load(s0 + j, wi[:, :, c * C4:(c + 1) * C4], DT)
                    if layer == 0:
                        load_rwords(sp, 0, j)
                load(s0 + 4, wo[:, 4:8, :], 4)
                load(s0 + 5, wo[:, 0:4, :], 4)
                if layer == 0:
                    for j, (what, b) in enumerate(DENSE):
                        cut = slice(b * C4, (b + 1) * C4)
                        if what == "down":
                            load(MIX_LOADS + j, by_tile(d_down[0, cut]), 4)
                        else:
                            w = d_gate if what == "gate" else d_up
                            load(MIX_LOADS + j, by_tile(w[0])[:, :, cut], DT)

            def load_item(i, expert):
                views = {n: w[0, bass.ds(expert, 1)].rearrange("e (t p) n -> p (e t) n", p=P)
                         for n, w in (("gate", e_gate), ("up", e_up), ("down", e_down))}
                for j, (what, b) in enumerate(EXPERT):
                    src = views[what]
                    src = src[:, 4 * b:4 * b + 4, :] if what == "down" else src[:, :, b * C4:(b + 1) * C4]
                    n = 4 if what == "down" else DT
                    sp.wait_ge(split_ready, i * PH + MH + 2 * load_before(j) + 2)
                    slot = slot_of(MOE0 + j)[0]
                    sp.dma_start(slot_buffer(slot).rearrange("p (t n) -> p t n", t=n), src).then_inc(
                        w_landed[slot], 16)

            sp.wait_ge(scored, GROUPS * DEPTH)
            with sp.Fori(0, NE) as e:
                load_item(e, e)
            sp.wait_ge(plan_ready, 1)
            extra = sp.value_load(plan[0:1, 7:8], min_val=0, max_val=EXTRA)
            with sp.Fori(0, EXTRA) as n:
                with sp.If(n < extra):
                    expert = sp.value_load(plan[0:1, bass.ds(n, 1)], min_val=0, max_val=NE - 1)
                    load_item(n + NE, expert)
            for t in range(NT):
                sp.wait_ge(h_ready, 2 * 3 + t + 1)
                sp.dma_start(out[0, t * P:(t + 1) * P, :], h[:, t, :]).then_inc(out_landed, 16)
            sp.wait_ge(out_landed, 16 * NT)

        @block.gpsimd
        def _(pool):
            steps = [0]

            def link(ins):
                steps[0] += 1
                ins.then_inc(pool_step, 1)
                pool.wait_ge(pool_step, steps[0])

            def load_gpre(n):
                src = (mix_pre if n % 2 == 0 else ffn_pre)[n // 2]
                if n:
                    pool.wait_ge(hs_ready, 2 * n)
                pool.dma_start(gpre[:, :], src.partition_broadcast(P)).then_inc(gpre_landed, 16)

            def load_gpost(n):
                src = (mix_post if n % 2 == 0 else ffn_post)[n // 2]
                if n:
                    pool.wait_ge(h_ready, 2 * n)
                pool.dma_start(gpost[:, :], src.partition_broadcast(P)).then_inc(gpost_landed, 16)

            def build_bias(layer):
                for quarter in range(4):
                    n = 4 * layer + quarter
                    pool.wait_ge(rwords_landed[layer][quarter % 2], 64 * (quarter // 2 + 1))
                    for b in range(2):
                        at = rwords[n % 2][:, 8 - 8 * b:]
                        words = bass.AP(at.tensor, at.offset,
                                        [list(at.ap[0]), [RPB_H, 4], [RPB_R, ROWS], [1, WIN]])
                        m = mask[:, b, :].unsqueeze(1).unsqueeze(1).broadcast_to([P, 4, ROWS, WIN])
                        pool.tensor_tensor(biasv[:, 4 * quarter:4 * quarter + 4, b], words, m, ALU.add).then_inc(
                            bias_part, 1)
                    if layer and quarter < 2:
                        load_rwords(pool, layer, quarter + 2)

            def window_means(layer):
                pool.wait_ge(fill_act, 4 * layer + 4)
                for g in range(3):
                    if g == 2:
                        pool.wait_ge(fill_dve, 4 * layer + 4)
                    window_delta(pool, link, layer, g, (win_a, win_b)).then_inc(delta_ready, 1)
                    pool.wait_ge(delta_ready, 3 * layer + g + 1)

            def plan_items():
                def f(c, n):
                    return rt[:, c:c + n]

                def te(ap):
                    return ap.rearrange("p (t e) -> p t e", t=NT)

                gates, pos, cnt = f(80, 16), f(96, 16), f(112, 8)
                extras, base, inc, tmp8 = f(120, 8), f(128, 8), f(136, 8), f(216, 8)
                rho, slots, item, tmp = f(144, 16), f(160, 16), f(176, 16), f(192, 16)
                row = f(208, 8)
                big = f(256, 64).rearrange("p (e f) -> p e f", e=NE)

                def sum_last(dst, src, n):
                    while n > 2:
                        n //= 2
                        lo, hi = (src[..., 0:n], src[..., n:2 * n])
                        link(pool.tensor_tensor(lo, lo, hi, ALU.add))
                    link(pool.tensor_tensor(dst, src[..., 0:1], src[..., 1:2], ALU.add))

                pool.wait_ge(slots_ready, 1)
                link(pool.tensor_scalar(extras, cnt, CAP + 0.5, None, ALU.is_gt))
                link(pool.tensor_scalar(rho, pos, CAP - 0.5, None, ALU.is_gt))
                k = 2
                while k * CAP < S:
                    link(pool.tensor_scalar(tmp8, cnt, k * CAP + 0.5, None, ALU.is_gt))
                    link(pool.tensor_tensor(extras, extras, tmp8, ALU.add))
                    link(pool.tensor_scalar(tmp, pos, k * CAP - 0.5, None, ALU.is_gt))
                    link(pool.tensor_tensor(rho, rho, tmp, ALU.add))
                    k += 1
                link(pool.tensor_tensor(big, before, extras.unsqueeze(1).broadcast_to([P, NE, NE]), ALU.mult))
                sum_last(base.unsqueeze(2), big, NE)
                link(pool.tensor_tensor(inc, base, extras, ALU.add))
                link(pool.tensor_scalar(slots, rho, -float(CAP), 1.0, ALU.mult, ALU.add))
                link(pool.tensor_tensor(slots, slots, pos, ALU.add))
                link(pool.tensor_tensor(te(item), te(rho), base.unsqueeze(1).broadcast_to([P, NT, NE]), ALU.add))
                link(pool.tensor_scalar(tmp, rho, 0.5, None, ALU.is_gt))
                link(pool.tensor_tensor(item, item, tmp, ALU.mult))
                own = f(256, 16)
                for n in range(EXTRA):
                    for src, dst in ((slots, item_pos), (gates, item_gate)):
                        link(pool.tensor_scalar(own, item, float(n + 1), None, ALU.is_equal))
                        link(pool.tensor_tensor(own, own, src, ALU.mult))
                        sum_last(dst[:, :, NE + n:NE + n + 1], te(own), NE)
                    link(pool.tensor_scalar(tmp8, inc, n + 0.5, None, ALU.is_lt))
                    sum_last(row[:, n:n + 1], tmp8, NE)
                link(pool.tensor_scalar(item_pos[:, :, NE:ITEMS], item_pos[:, :, NE:ITEMS], -1.0, None, ALU.add))
                if EXTRA < 7:
                    link(pool.memset(row[:, EXTRA:7], 0.0))
                link(pool.tensor_scalar(row[:, 0:7], row[:, 0:7], float(NE - 1), None, ALU.min))
                link(pool.tensor_copy(row[:, 7:8], inc[:, 7:8]))
                for a, pad in ((item_pos, -1.0), (item_gate, 0.0)):
                    link(pool.memset(a[:, :, ITEMS], pad))
                pool.tensor_copy(plan[0:1, :], row[0:1, :]).then_inc(plan_ready, 1)

            load_gpre(0)
            pool.dma_start(rows[:, :], pool_scale.rearrange("l (t p) -> (l t) p", p=P)).then_inc(rows_landed, 16)
            link(pool.memset(uT[:, :, :], 0.0))
            for layer in range(DEPTH):
                if layer:
                    pool.wait_ge(pmix_done, layer)
                pool.dma_start(poolw[:, :, :], pool_w[layer].rearrange("g c d -> c g d")).then_inc(poolw_landed, 16)
                if layer == 0:
                    pool.wait_ge(cst_landed, 16)
                    build_bias(0)
                    load_gpost(0)
                    load_gpre(1)
                    pool.dma_start(router_sb[:, :, :], router[0].rearrange("(t p) e -> p t e", p=P)).then_inc(
                        router_landed, 16)
                window_means(layer)
                load_gpost(2 * layer + 1)
                if layer == 0:
                    load_gpre(2)
                    load_rwords(pool, 1, 0)
                    load_rwords(pool, 1, 1)
                    build_bias(1)
                    load_gpost(2)
                    load_gpre(3)
            pool.wait_ge(half_done, MH)
            pool.memset(spread[:, :], 0.0)
            pool.memset(ynat[:, C4:2 * C4], 0.0).then_inc(ynat_act, 1)
            pool.memset(ynat[:, 0:C4], 0.0).then_inc(ynat_dve, 1)
            pool.memset(facc[:, :, :].rearrange("p t n -> p (t n)"), 0.0).then_inc(facc_done, 4)
            plan_items()
            pool.wait_ge(hs_hi_ready, 1)
            pool.tensor_tensor(hs_lo[:, :, :], hs[:, :, :], hs_hi[:, :, :].bitcast(F32), ALU.subtract).then_inc(
                hs_split, 1)

        @block.tensor
        def _(pe):
            mm = pe.matmul

            def product(dst, still, moving, start, stop):
                mm(dst, still[0], moving[0], start=start, stop=False)
                mm(dst, still[0], moving[1], start=False, stop=False)
                return mm(dst, still[1], moving[0], start=False, stop=stop)

            def split_half(n, item=None):
                pe.wait_ge(split_ready, n + 1 if item is None else item * PH + n + 1)
                return w_hi[:, n % STAGE, :], w_lo[:, n % STAGE, :]

            def transposes(n):
                for t in range(NT):
                    pe.wait_ge(hs_ready, 2 * n + t + 1)
                    bank = (pc, pd)[t]
                    for dt in range(DT):
                        ins = pe.transpose(bank[:, dt * P:(dt + 1) * P], hs[:, t, dt * P:(dt + 1) * P], ident)
                        if dt % 4 == 3:
                            ins.then_inc(hs_tp, 1)
                pe.wait_ge(hT_ready, 4 * n + 3)

            def mixing(layer):
                h0 = 2 * mixing_first_load(layer)

                def fill(f, part):
                    if part == 0 and f >= 2:
                        pe.wait_ge((fill_act, fill_dve)[f % 2], 4 * layer + f // 2)
                    parts = [w.rearrange("p (t n) -> p t n", t=DT) for w in split_half(h0 + f)]
                    dst = pc[:, (f % 2) * C4 + part * C2:(f % 2) * C4 + (part + 1) * C2]
                    for dt in range(DT):
                        if (f, part, dt) == (0, 0, 4):
                            pe.wait_ge(hT_ready, 4 * (2 * layer + 1))
                        tok = (hT_hi[:, dt, :], hT_lo[:, dt, :])
                        if f in (4, 5):
                            still = [a[:, part * P:(part + 1) * P] for a in tok]
                            moving = [w[:, dt, :] for w in parts]
                        else:
                            still = [w[:, dt, part * P:(part + 1) * P] for w in parts]
                            moving = tok
                        ins = product(dst, still, moving, dt == 0, dt == DT - 1)
                    if part == 1:
                        ins.then_inc(half_done, 1)

                def scores(g):
                    b, rho = g // 4, g % 4
                    if g == 0:
                        pe.wait_ge(fill_act, 4 * layer + 2)
                        pe.wait_ge(fill_dve, 4 * layer + 2)
                    else:
                        pe.wait_ge(scored, GROUPS * layer + g)
                    rows32 = slice(HD * rho, HD * (rho + 1))
                    for m in range(4):
                        q = qT[rows32, m, b * P:(b + 1) * P]
                        k = kT[rows32, m, :].rearrange("p (r c) -> p r c", r=ROWS)[:, :, WIN0 * b:WIN0 * b + WIN]
                        ins = mm(pa[:, m * 256:m * 256 + ROWS * WIN], q, k, start=True, stop=True)
                    ins.then_inc(qk_done, 1)

                def turn(g):
                    pe.wait_ge(prob_ready, GROUPS * layer + g + 1)
                    if g or layer:
                        pe.wait_ge(pt_dve, GROUPS * layer + g)
                        pe.wait_ge(pt_act, GROUPS * layer + g)
                    for kt in range(2):
                        for m in range(4):
                            ins = pe.transpose(pb[:, kt * C4 + m * P:kt * C4 + (m + 1) * P],
                                               prob[:, g % 2, m, 2 * kt:2 * kt + 2, :].rearrange("p i j -> p (i j)"),
                                               ident)
                        ins.then_inc((tp0_done, tp1_done)[kt], 1)

                def values(g):
                    b, rho = g // 4, g % 4
                    pe.wait_ge(pt_dve, GROUPS * layer + g + 1)
                    pe.wait_ge(pt_act, GROUPS * layer + g + 1)
                    if g == 0:
                        pe.wait_ge(fill_act, 4 * layer + 3)
                        pe.wait_ge(fill_dve, 4 * layer + 3)
                    for m in range(4):
                        c = (4 * m + rho) * HD
                        for kt in range(2):
                            ins = mm(pd[HD * rho:HD * (rho + 1), b * C4 + m * P:b * C4 + (m + 1) * P],
                                     vv[:, kt, c:c + HD], pt(g % 4)[:, kt, m, :], start=kt == 0, stop=kt == 1)
                    ins.then_inc(pv_done, 1)

                def project(half, src):
                    parts = [w.rearrange("p (t n) -> p t n", t=2) for w in split_half(h0 + 8 + half)]

                    def products(et, t):
                        e = 2 * (half % 2) + et
                        still = [a[:, e, t * P:(t + 1) * P] for a in src]
                        for j in range(2):
                            ins = product((pa, pb)[t][:, j * C4:(j + 1) * C4], still,
                                          [w[:, et, j * C4:(j + 1) * C4] for w in parts],
                                          half == 0 and et == 0, half == 3 and et == 1)
                        return ins

                    if half < 3:
                        for et in range(2):
                            for t in range(NT):
                                ins = products(et, t)
                    else:
                        products(0, 0)
                        products(1, 0).then_inc(tile0_done, 1)
                        products(0, 1)
                        ins = products(1, 1)
                    ins.then_inc(half_done, 1)

                if layer == 0:
                    pe.wait_ge(rows_landed, 16)
                    pe.transpose(pb[:, 0:8], rows[:, :], ident[0:8, 0:8]).then_inc(cols_tp, 1)
                for f in range(4):
                    fill(f, 0)
                    fill(f, 1)
                pe.wait_ge(cols_ready, 1)
                for g in range(GROUPS):
                    scores(g)
                    if g:
                        turn(g - 1)
                    fill(4 + g // 2, g % 2)
                    if g == 4:
                        values(0)
                        values(1)
                    elif g == 5:
                        values(2)
                        values(3)
                    elif g > 5:
                        values(g - 2)
                turn(7)
                values(6)
                values(7)
                pe.wait_ge(yaT_ready, 2 * (layer + 1))
                project(0, (yaT_hi, yaT_lo))
                pe.wait_ge(poolw_landed, 16 * (layer + 1))
                pe.wait_ge(fill_act, 4 * layer + 4)
                pe.wait_ge(fill_dve, 4 * layer + 4)
                pe.wait_ge(delta_ready, 3 * (layer + 1))
                pe.wait_ge(delta_dve_ready, layer + 1)
                for g in range(4):
                    ins = mm(pc[:, g * S:(g + 1) * S], poolw[:, g, :], delta[:, g, :], start=True, stop=True)
                ins.then_inc(pmix_done, 1)
                project(1, (yaT_hi, yaT_lo))
                pe.wait_ge(ypT_ready, layer + 1)
                project(2, (ypT_hi, ypT_lo))
                project(3, (ypT_hi, ypT_lo))

            def dense():
                h0 = 2 * MIX_LOADS
                for j, (what, b) in enumerate(DENSE):
                    for c in range(2):
                        parts = split_half(h0 + 2 * j + c)
                        if what == "down":
                            parts = [w.rearrange("p (t n) -> p t n", t=2) for w in parts]
                            pe.wait_ge(dhid_ready, 2 * b + c + 1)
                            for t in range(NT):
                                for f in range(2):
                                    still = [a[:, 2 * c + f, t * P:(t + 1) * P] for a in (dhid_hi, dhid_lo)]
                                    for n in range(2):
                                        ins = product((pa, pb)[t][:, n * C4:(n + 1) * C4], still,
                                                      [w[:, f, n * C4:(n + 1) * C4] for w in parts],
                                                      b == 0 and c == 0 and f == 0,
                                                      b == DBLOCKS - 1 and c == 1 and f == 1)
                                if (b, c, t) == (DBLOCKS - 1, 1, 0):
                                    ins.then_inc(tile0_done, 1)
                        else:
                            parts = [w.rearrange("p (t n) -> p t n", t=DT) for w in parts]
                            if b:
                                pe.wait_ge(dsilu_ready if what == "gate" else dprod_ready, 2 * (b - 1) + c + 1)
                            bank = (pc if what == "gate" else pd)[:, c * C4:(c + 1) * C4]
                            for f in range(2):
                                for dt in range(DT):
                                    if (j, c, f, dt) == (0, 0, 0, 4):
                                        pe.wait_ge(hT_ready, 4 * 2)
                                    ins = product(bank[:, f * S:(f + 1) * S], [w[:, dt, f * P:(f + 1) * P] for w in parts],
                                                  (hT_hi[:, dt, :], hT_lo[:, dt, :]), dt == 0, dt == DT - 1)
                        ins.then_inc(half_done, 1)

            def routing():
                pe.wait_ge(router_ready, 1)
                for dt in range(DT):
                    if dt == 4:
                        pe.wait_ge(hT_ready, 4 * 4)
                    for w in (router_hi, router_lo):
                        for part in (hT_hi, hT_lo):
                            ins = mm(pb[0:NE, 0:S], w[:, dt, :], part[:, dt, :], start=dt == 0 and w is router_hi
                                     and part is hT_hi, stop=dt == DT - 1 and w is router_lo and part is hT_lo)
                ins.then_inc(logits_done, 1)
                pe.wait_ge(lgT_ready, 1)
                for t in range(NT):
                    ins = pe.transpose(pa[:, t * NE:(t + 1) * NE], lgT[:, t * P:(t + 1) * P], ident[0:NE, 0:NE])
                ins.then_inc(logits_tp, 1)
                pe.wait_ge(sel_ready, 1)
                sel = rt[:, 16:32].rearrange("p (t e) -> p t e", t=NT)
                mm(pb[:, C4:C4 + NE], tri, sel[:, 0], start=True, stop=True)
                mm(pb[:, C4 + NE:C4 + 2 * NE], ones, sel[:, 0], start=True, stop=False)
                mm(pb[:, C4 + NE:C4 + 2 * NE], tri, sel[:, 1], start=False, stop=True).then_inc(count_done, 1)
                mm(pa[:, 2 * NE:3 * NE], ones, sel[:, 0], start=True, stop=False)
                mm(pa[:, 2 * NE:3 * NE], ones, sel[:, 1], start=False, stop=True).then_inc(count_done, 1)

            def gather(i, split):
                pe.wait_ge(pick_ready, i + 1)
                pe.wait_ge(facc_done, i * 4 + 4)
                for j in range(2):
                    cut = slice(j * C4, (j + 1) * C4)
                    for t in range(NT):
                        if split:
                            mm(pa[0:CAP, cut], pick[:, t, :], hs_hi[:, t, cut], start=t == 0, stop=False)
                            ins = mm(pa[0:CAP, cut], pick[:, t, :], hs_lo[:, t, cut], start=False, stop=t == NT - 1)
                        else:
                            ins = mm(pa[0:CAP, cut], pick[:, t, :].bitcast(F32), hs[:, t, cut],
                                     start=t == 0, stop=t == NT - 1)
                ins.then_inc(gather_done, 1)

            def turn_tokens(i):
                pe.wait_ge(xnat_dve, i + 1)
                pe.wait_ge(xnat_act, i + 1)
                for dt in range(DT):
                    at = dt // 4 * C4 + dt % 4 * CAP
                    ins = pe.transpose(pa[:, at:at + CAP], xnat[0:CAP, dt * P:(dt + 1) * P], ident[0:CAP, 0:CAP])
                ins.then_inc(xT_tp, 1)

            def combine(i, t):
                if t == 0:
                    pe.wait_ge(ynat_dve, i + 1)
                    pe.wait_ge(ynat_act, i + 1)
                for j in range(2):
                    pe.wait_ge(facc_done, i * 4 + 4 + 2 * t + j - 1)
                    mm(pa[:, j * C4:(j + 1) * C4], spread[0:CAP, t * P:(t + 1) * P],
                       ynat[0:CAP, j * C4:(j + 1) * C4], start=True, stop=True).then_inc(comb_done, 1)

            def expert_pass(i):
                def turn_hidden(b):
                    pe.wait_ge(ehid_ready, i * EBLOCKS + b + 1)
                    if b:
                        pe.wait_ge(eT_ready, i * EBLOCKS + b)
                    for f in range(4):
                        ins = pe.transpose(pb[:, f * CAP:(f + 1) * CAP], ehid[0:CAP, f * P:(f + 1) * P],
                                           ident[0:CAP, 0:CAP])
                    ins.then_inc(eT_tp, 1)

                pe.wait_ge(xT_ready, i + 1)
                for j, (what, b) in enumerate(EXPERT):
                    for c in range(2):
                        parts = split_half(MH + 2 * j + c, i)
                        if what == "down":
                            parts = [w.rearrange("p (t n) -> p t n", t=2) for w in parts]
                            if c == 0:
                                pe.wait_ge(eT_ready, i * EBLOCKS + b + 1)
                            for f in range(2):
                                still = [a[:, b % 2, 2 * c + f, :] for a in (eT_hi, eT_lo)]
                                for n in range(2):
                                    ins = product(pd[0:CAP, n * C4:(n + 1) * C4], still,
                                                  [w[:, f, n * C4:(n + 1) * C4] for w in parts],
                                                  b == 0 and c == 0 and f == 0,
                                                  b == EBLOCKS - 1 and c == 1 and f == 1)
                        else:
                            parts = [w.rearrange("p (t n) -> p t n", t=DT) for w in parts]
                            if b and c == 0:
                                pe.wait_ge(esilu_ready if what == "gate" else ehid_ready, i * EBLOCKS + b)
                            at = (0 if what == "gate" else C4) + c * C2
                            for dt in range(DT):
                                ins = product(pc[0:CAP, at:at + C2], (xT_hi[:, dt, :], xT_lo[:, dt, :]),
                                              [w[:, dt, :] for w in parts], dt == 0, dt == DT - 1)
                        ins.then_inc(half_done, 1)
                        if what == "gate" and b and c == 0:
                            turn_hidden(b - 1)
                        if (what, b, c) == ("down", EBLOCKS - 2, 0):
                            turn_hidden(EBLOCKS - 1)
                        if (what, b, c) == ("gate", 0, 1):
                            combine(i, 0)
                        if (what, b, c) == ("up", 0, 0):
                            combine(i, 1)
                    if (what, b) == ("up", 0):
                        for t in range(NT):
                            ins = pe.transpose(pb[0:CAP, C4 + t * P:C4 + (t + 1) * P], gpick[:, t, :], ident)
                        ins.then_inc(spread_tp, 1)
                    if (what, b) == ("down", 2):
                        pe.wait_ge(hs_split, 1)
                        gather(i + 1, True)
                    if (what, b) == ("down", 3):
                        turn_tokens(i + 1)

            pe.wait_ge(cst_landed, 16)
            transposes(0)
            mixing(0)
            transposes(1)
            dense()
            transposes(2)
            mixing(1)
            transposes(3)
            routing()
            gather(0, False)
            turn_tokens(0)
            with pe.Fori(0, NE) as i:
                expert_pass(i)
            extra = pe.value_load(plan[0:1, 7:8], min_val=0, max_val=EXTRA)
            with pe.Fori(0, EXTRA) as n:
                with pe.If(n < extra):
                    expert_pass(n + NE)
            for t in range(NT):
                combine(extra + NE, t)

        @block.scalar
        def _(act):
            counts = {"split": 0, "squares": 0}

            def split_to(n):
                while counts["split"] < n:
                    k = counts["split"]
                    seq, c = k // 2, k % 2
                    if k == 0:
                        act.wait_ge(half_landed, 16)
                    elif c == 0 or k == 1:
                        act.wait_ge(w_landed[seq % RING], 16 * (seq // RING + 1))
                    if k >= STAGE:
                        act.wait_ge(half_done, k - STAGE + 1)
                    src, hi, _ = halves(seq, rows_first(seq))[c]
                    act.activation(hi, src, ACT.Copy).then_inc(hi_ready, 1)
                    counts["split"] += 1

            def rms(dst, src, c):
                counts["squares"] += 1
                s = st[:, c:c + 1]
                act.activation(dst, src, ACT.Square, accum_out=s).then_inc(squares, 1)
                act.wait_ge(squares, counts["squares"])
                return act.activation(s, s, ACT.Sqrt, scale=1.0 / D, bias=cst[:, K_EPS:K_EPS + 1])

            def pre_norm(n):
                for t in range(NT):
                    if n == 0:
                        act.wait_ge(x_landed, 16)
                    else:
                        act.wait_ge(h_ready, 2 * (n - 1) + t + 1)
                    rms(hs[:, t, :], h[:, t, :], 2 * n + t).then_inc(rms_pre, 1)
                for t in range(NT):
                    for k in range(2):
                        act.wait_ge(hs_tp, 4 * n + 2 * t + k + 1)
                        act.activation(hT_hi[:, 4 * k:4 * k + 4, t * P:(t + 1) * P],
                                       (pc, pd)[t][:, k * C4:(k + 1) * C4].rearrange("p (a n) -> p a n", a=4),
                                       ACT.Copy).then_inc(hT_hi_ready, 1)

            def post_norm(n, value):
                act.preload_act_table(ACT.Sqrt)
                for t in range(NT):
                    if n == 3:
                        act.wait_ge(facc_done, value + 2 * t + 2)
                    elif t == 0:
                        act.wait_ge(tile0_done, n + 1)
                    else:
                        act.wait_ge(half_done, value)
                    if n == 1:
                        act.wait_ge(bias_part, 8 * DEPTH)
                    src = facc[:, t, :] if n == 3 else (pa, pb)[t][:, :]
                    rms(pt23[:, t, :], src, 8 + 2 * n + t).then_inc(rms_post, 1)

            def mixing(layer):
                h0 = 2 * mixing_first_load(layer)

                def fill_q():
                    act.wait_ge(half_done, h0 + 1)
                    for m in range(2):
                        dst = qT[:, m, :].rearrange("p (b r c) -> p r b c", b=2, r=ROWS)
                        ins = act.activation(dst, query_order(pc[:, m * S:(m + 1) * S]), ACT.Copy, scale=HD ** -0.5)
                    ins.then_inc(fill_act, 1)

                def fill(f, dst):
                    act.wait_ge(half_done, h0 + f + 1)
                    act.activation(dst, pc[:, 0:C4].rearrange("p (a n) -> p a n", a=2), ACT.Copy).then_inc(fill_act, 1)

                def exps(g):
                    b = g // 4
                    act.wait_ge(negmax_ready, GROUPS * layer + g + 1)
                    for m in range(4):
                        p = prob[:, g % 2, m, :, WIN0 * b:WIN0 * b + WIN]
                        ins = act.activation(p, p, ACT.Exp, bias=negmax[:, g % 2, m:m + 1],
                                             accum_out=sums[:, g % 2, m:m + 1])
                    ins.then_inc(exp_done, 1)

                def probs_out(g):
                    act.wait_ge(tp1_done, GROUPS * layer + g + 1)
                    if g >= 4:
                        act.wait_ge(pv_done, GROUPS * layer + g - 3)
                    act.activation(pt(g % 4)[:, 1], pb[:, C4:2 * C4].rearrange("p (m q) -> p m q", m=4),
                                   ACT.Copy).then_inc(pt_act, 1)

                split_to(h0 + 3)
                act.preload_act_table(ACT.Exp)
                fill_q()
                split_to(h0 + 5)
                fill(2, kT[:, 0:2, :])
                split_to(h0 + 6)
                for g in range(GROUPS):
                    exps(g)
                    if g:
                        probs_out(g - 1)
                    if g == 1:
                        fill(4, vv[:, :, 0:C2])
                    if g == 5:
                        fill(6, uT[:, 0:2, POOL_PAD:POOL_PAD + S])
                    if g % 2:
                        split_to(h0 + 7 + g // 2)
                probs_out(7)
                for b in range(2):
                    act.wait_ge(pv_done, GROUPS * layer + 4 * (b + 1))
                    dst = yaT_hi[:, :, :].rearrange("p e (r c) -> p (e r) c", r=ROWS)[:, :, QC * b:QC * (b + 1)]
                    act.activation(dst, token_order(pd[:, b * C4:(b + 1) * C4]), ACT.Copy).then_inc(yaT_hi_ready, 1)
                split_to(h0 + 11)
                if layer:
                    act.wait_ge(router_landed, 16)
                    act.activation(router_hi[:, :, :], router_sb[:, :, :], ACT.Copy).then_inc(router_hi_ready, 1)
                else:
                    act.wait_ge(cols_ready, 1)
                act.wait_ge(pmix_done, layer + 1)
                for g in range(4):
                    c = 4 * layer + g
                    ins = act.activation(ypT_hi[:, g, :], pc[:, g * S:(g + 1) * S], ACT.Copy, scale=cols[:, c:c + 1])
                ins.then_inc(ypT_hi_ready, 1)
                split_to(h0 + 14 if layer == 0 else h0 + 12)

            def dense():
                h0 = 2 * MIX_LOADS
                for j, (what, b) in enumerate(DENSE):
                    for c in range(2):
                        k = h0 + 2 * j + c
                        split_to(k + 3)
                        if what == "gate":
                            act.wait_ge(half_done, k + 1)
                            if b:
                                act.wait_ge(dhid_ready, 2 * (b - 1) + c + 1)
                            act.activation(dsilu[:, c, :], pc[:, c * C4:(c + 1) * C4], ACT.Silu).then_inc(
                                dsilu_ready, 1)
                        elif what == "up":
                            act.wait_ge(dprod_ready, 2 * b + c + 1)
                            act.activation(dhid_hi[:, 2 * c:2 * c + 2, :],
                                           dsilu[:, c, :].rearrange("p (f n) -> p f n", f=2), ACT.Copy).then_inc(
                                dhid_hi_ready, 1)

            def expert_split(i, k):
                seq, c = MOE0 + k // 2, k % 2
                if c == 0:
                    slot, nth = slot_of(seq)
                    act.wait_ge(w_landed[slot], i * (16 * slot_loads(slot)) + 16 * nth)
                act.wait_ge(half_done, i * PH + MH + k - STAGE + 1)
                src, hi, _ = halves(seq, EXPERT[k // 2][0] == "down")[c]
                act.activation(hi, src, ACT.Copy).then_inc(hi_ready, 1)

            def tokens_in(i):
                act.wait_ge(half_done, i * PH + MH - 4)
                act.wait_ge(xT_tp, i + 1)
                act.activation(xT_hi[:, :, :].rearrange("p (b t) n -> p b (t n)", b=2),
                               pa[:, :].rearrange("p (b n) -> p b n", b=2)[:, :, 0:4 * CAP], ACT.Copy).then_inc(
                    xT_hi_ready, 1)

            def tokens_gathered(i):
                act.wait_ge(gather_done, i + 1)
                act.activation(xnat[0:CAP, C4:2 * C4], pa[0:CAP, C4:2 * C4], ACT.Copy).then_inc(xnat_act, 1)

            def expert_pass(i, first, last):
                ahead = [first]

                def split_until(k):
                    while ahead[0] < min(k, last):
                        if ahead[0] < PH:
                            expert_split(i, ahead[0])
                        else:
                            expert_split(i + 1, ahead[0] - PH)
                        ahead[0] += 1

                def hidden_turned(b):
                    act.wait_ge(eT_tp, i * EBLOCKS + b + 1)
                    act.activation(eT_hi[:, b % 2].rearrange("p f n -> p (f n)"), pb[:, 0:4 * CAP],
                                   ACT.Copy).then_inc(eT_hi_ready, 1)

                for j, (what, b) in enumerate(EXPERT):
                    for c in range(2):
                        k = 2 * j + c
                        split_until(k + 3)
                        if what == "gate" and c == 0 and b:
                            hidden_turned(b - 1)
                        if (what, b, c) == ("down", EBLOCKS - 2, 0):
                            hidden_turned(EBLOCKS - 1)
                        if what == "gate" and c == 1:
                            act.wait_ge(half_done, i * PH + MH + k + 1)
                            if b:
                                act.wait_ge(eT_tp, i * EBLOCKS + b)
                            act.activation(ehid[0:CAP, :], pc[0:CAP, 0:C4], ACT.Silu).then_inc(esilu_ready, 1)
                        if (what, b, c) == ("up", 0, 1):
                            act.wait_ge(spread_tp, i + 1)
                            act.activation(spread[0:CAP, :], pb[0:CAP, C4:C4 + S], ACT.Copy).then_inc(spread_ready, 1)
                        if (what, b, c) == ("down", 2, 1):
                            tokens_gathered(i + 1)
                        if (what, b, c) == ("up", EBLOCKS - 1, 1):
                            tokens_in(i + 1)
                act.wait_ge(half_done, i * PH + MH + PH)
                act.activation(ynat[0:CAP, C4:2 * C4], pd[0:CAP, C4:2 * C4], ACT.Copy).then_inc(ynat_act, 1)
                split_until(PH + 3)

            act.preload_act_table(ACT.Sqrt)
            act.wait_ge(cst_landed, 16)
            pre_norm(0)
            mixing(0)
            post_norm(0, 2 * MIX_LOADS)
            pre_norm(1)
            act.preload_act_table(ACT.Silu)
            dense()
            post_norm(1, 2 * (MIX_LOADS + DENSE_LOADS))
            pre_norm(2)
            mixing(1)
            post_norm(2, MH)
            pre_norm(3)
            for k in range(2):
                expert_split(0, k)
            act.wait_ge(lshift_ready, 1)
            act.activation(rt[:, 48:64], rt[:, 32:48], ACT.Exp).then_inc(lexp_done, 1)
            act.preload_act_table(ACT.Silu)
            expert_split(0, 2)
            tokens_gathered(0)
            tokens_in(0)
            act.activation(hs_hi[:, :, :], hs[:, :, :], ACT.Copy).then_inc(hs_hi_ready, 1)
            with act.Fori(0, NE - 1) as i:
                expert_pass(i, 3, PH + 3)
            expert_pass(NE - 1, 3, PH)
            act.wait_ge(plan_ready, 1)
            extra = act.value_load(plan[0:1, 7:8], min_val=0, max_val=EXTRA)
            with act.Fori(0, EXTRA) as n:
                with act.If(n < extra):
                    expert_pass(n + NE, 0, PH)
            post_norm(3, extra * 4 + 4 * NE + 4)

        @block.vector
        def _(dve):
            counts = {"step": 0, "split": 0}

            def link(ins):
                counts["step"] += 1
                ins.then_inc(dve_step, 1)
                dve.wait_ge(dve_step, counts["step"])

            def split_to(n):
                while counts["split"] < n:
                    k = counts["split"]
                    dve.wait_ge(hi_ready, k + 1)
                    src, hi, lo = halves(k // 2, rows_first(k // 2))[k % 2]
                    dve.tensor_tensor(lo, src, hi.bitcast(F32), ALU.subtract).then_inc(split_ready, 1)
                    counts["split"] += 1

            def rms_inverse(c):
                link(dve.reciprocal(st[:, c:c + 1], st[:, c:c + 1]))

            def pre_norm(n):
                dve.wait_ge(gpre_landed, 16 * (n + 1))
                for t in range(NT):
                    dve.wait_ge(rms_pre, 2 * n + t + 1)
                    rms_inverse(2 * n + t)
                    dve.scalar_tensor_tensor(out=hs[:, t, :], in0=h[:, t, :], scalar=st[:, 2 * n + t:2 * n + t + 1],
                                             in1=gpre[:, :], op0=ALU.mult, op1=ALU.mult).then_inc(hs_ready, 1)
                for t in range(NT):
                    for k in range(2):
                        dve.wait_ge(hT_hi_ready, 4 * n + 2 * t + k + 1)
                        part = (slice(None), slice(4 * k, 4 * k + 4), slice(t * P, (t + 1) * P))
                        dve.tensor_tensor(hT_lo[part],
                                          (pc, pd)[t][:, k * C4:(k + 1) * C4].rearrange("p (a n) -> p a n", a=4),
                                          hT_hi[part].bitcast(F32), ALU.subtract).then_inc(hT_ready, 1)

            def post_norm(n, value):
                dve.wait_ge(gpost_landed, 16 * (n + 1))
                for t in range(NT):
                    if n == 3:
                        dve.wait_ge(facc_done, value + 2 * t + 2)
                    elif t == 0:
                        dve.wait_ge(tile0_done, n + 1)
                    else:
                        dve.wait_ge(half_done, value)
                    if n < 3:
                        dve.wait_ge(squares, 4 * n + 3 + t)
                    src = facc[:, t, :] if n == 3 else (pa, pb)[t][:, :]
                    link(dve.tensor_tensor(hs[:, t, :], src, gpost[:, :], ALU.mult))
                    dve.wait_ge(rms_post, 2 * n + t + 1)
                    rms_inverse(8 + 2 * n + t)
                    dve.scalar_tensor_tensor(out=h[:, t, :], in0=hs[:, t, :], scalar=st[:, 8 + 2 * n + t:9 + 2 * n + t],
                                             in1=h[:, t, :], op0=ALU.mult, op1=ALU.add).then_inc(h_ready, 1)

            def mixing(layer):
                h0 = 2 * mixing_first_load(layer)

                def fill_q():
                    dve.wait_ge(half_done, h0 + 2)
                    for m in range(2, 4):
                        dst = qT[:, m, :].rearrange("p (b r c) -> p r b c", b=2, r=ROWS)
                        ins = dve.tensor_scalar(dst, query_order(pc[:, m * S:(m + 1) * S]), HD ** -0.5, None, ALU.mult)
                    ins.then_inc(fill_dve, 1)

                def fill(f, dst):
                    dve.wait_ge(half_done, h0 + f + 1)
                    dve.tensor_copy(dst, pc[:, C4:2 * C4].rearrange("p (a n) -> p a n", a=2)).then_inc(fill_dve, 1)

                def add_bias(g):
                    b, rho = g // 4, g % 4
                    if g == 0:
                        dve.wait_ge(bias_part, 8 * (layer + 1))
                    if g >= 2:
                        dve.wait_ge(tp1_done, GROUPS * layer + g - 1)
                    if g % 4 < 2:
                        c = WIN if b == 0 else 0
                        dve.memset(prob[:, g % 2, :, :, c:c + COLS - WIN].rearrange("p m i j -> p (m i) j"), 0.0)
                    dve.wait_ge(qk_done, GROUPS * layer + g + 1)
                    win = prob[:, g % 2, :, :, WIN0 * b:WIN0 * b + WIN]
                    sc = pa[:, :].rearrange("p (m n) -> p m n", m=4)[:, :, 0:ROWS * WIN].rearrange(
                        "p m (i j) -> p m i j", i=ROWS)
                    bs = bias[:, :].rearrange("p (m r b i j) -> p m r b i j", m=4, r=4, b=2, i=ROWS)[:, :, rho, b]
                    dve.tensor_tensor(win, sc, bs, ALU.add).then_inc(scored, 1)
                    dve.wait_ge(scored, GROUPS * layer + g + 1)
                    nm = negmax[:, g % 2, :]
                    link(dve.tensor_reduce(nm, win, AX.XY, ALU.max))
                    dve.tensor_scalar(nm, nm, -1.0, None, ALU.mult).then_inc(negmax_ready, 1)

                def normalise(g):
                    win = prob[:, g % 2, :, :, WIN0 * (g // 4):WIN0 * (g // 4) + WIN]
                    r = rinv[:, g % 2, :]
                    dve.wait_ge(exp_done, GROUPS * layer + g + 1)
                    link(dve.reciprocal(r, sums[:, g % 2, :]))
                    for m in range(4):
                        ins = dve.tensor_scalar(win[:, m], win[:, m], r[:, m:m + 1], None, ALU.mult)
                    ins.then_inc(prob_ready, 1)

                def probs_out(g):
                    dve.wait_ge(tp0_done, GROUPS * layer + g + 1)
                    if g >= 4:
                        dve.wait_ge(pv_done, GROUPS * layer + g - 3)
                    dve.tensor_copy(pt(g % 4)[:, 0], pb[:, 0:C4].rearrange("p (m q) -> p m q", m=4)).then_inc(
                        pt_dve, 1)

                split_to(h0 + 3)
                if layer == 0:
                    dve.wait_ge(cols_tp, 1)
                    dve.tensor_copy(cols[:, :], pb[:, 0:8]).then_inc(cols_ready, 1)
                split_to(h0 + 4)
                fill_q()
                split_to(h0 + 6)
                fill(3, kT[:, 2:4, :])
                for g in range(GROUPS):
                    add_bias(g)
                    if g:
                        probs_out(g - 1)
                    if g % 2 == 0 and g:
                        split_to(h0 + 6 + g // 2)
                    normalise(g)
                    if g == 3:
                        fill(5, vv[:, :, C2:C4])
                fill(7, uT[:, 2:4, POOL_PAD:POOL_PAD + S])
                probs_out(7)
                for b in range(2):
                    dve.wait_ge(yaT_hi_ready, 2 * layer + b + 1)
                    cut = [a[:, :, :].rearrange("p e (r c) -> p (e r) c", r=ROWS)[:, :, QC * b:QC * (b + 1)]
                           for a in (yaT_lo, yaT_hi)]
                    dve.tensor_tensor(cut[0], token_order(pd[:, b * C4:(b + 1) * C4]), cut[1].bitcast(F32),
                                      ALU.subtract).then_inc(yaT_ready, 1)
                split_to(h0 + 10)
                dve.wait_ge(fill_dve, 4 * layer + 4)
                window_delta(dve, link, layer, 3, (win_c, win_d)).then_inc(delta_dve_ready, 1)
                split_to(h0 + 11)
                if layer:
                    dve.wait_ge(router_hi_ready, 1)
                    dve.tensor_tensor(router_lo[:, :, :], router_sb[:, :, :], router_hi[:, :, :].bitcast(F32),
                                      ALU.subtract).then_inc(router_ready, 1)
                dve.wait_ge(ypT_hi_ready, layer + 1)
                for g in range(4):
                    c = 4 * layer + g
                    ins = dve.scalar_tensor_tensor(out=ypT_lo[:, g, :], in0=pc[:, g * S:(g + 1) * S],
                                                   scalar=cols[:, c:c + 1], in1=ypT_hi[:, g, :].bitcast(F32),
                                                   op0=ALU.mult, op1=ALU.subtract)
                ins.then_inc(ypT_ready, 1)
                split_to(h0 + 14 if layer == 0 else h0 + 12)

            def dense():
                h0 = 2 * MIX_LOADS
                for j, (what, b) in enumerate(DENSE):
                    for c in range(2):
                        k = h0 + 2 * j + c
                        split_to(k + 3)
                        if what == "up":
                            dve.wait_ge(half_done, k + 1)
                            dve.wait_ge(dsilu_ready, 2 * b + c + 1)
                            buf = dsilu[:, c, :]
                            dve.tensor_tensor(buf, buf, pd[:, c * C4:(c + 1) * C4], ALU.mult).then_inc(dprod_ready, 1)
                            dve.wait_ge(dhid_hi_ready, 2 * b + c + 1)
                            dve.tensor_tensor(dhid_lo[:, 2 * c:2 * c + 2, :], buf.rearrange("p (f n) -> p f n", f=2),
                                              dhid_hi[:, 2 * c:2 * c + 2, :].bitcast(F32), ALU.subtract).then_inc(
                                dhid_ready, 1)

            def routing():
                def f(c, n):
                    return rt[:, c:c + n]

                def te(ap):
                    return ap.rearrange("p (t e) -> p t e", t=NT)

                lg, sel, sh, ex = f(0, 16), f(16, 16), f(32, 16), f(48, 16)
                m1, den = f(64, 2), f(66, 2)
                gates, pos, cnt = f(80, 16), f(96, 16), f(112, 8)
                big = f(256, 128).rearrange("p (t e f) -> p t e f", t=NT, e=NE)
                big2 = f(384, 128).rearrange("p (t e f) -> p t e f", t=NT, e=NE)
                rank = f(224, 16)
                dve.wait_ge(logits_done, 1)
                dve.tensor_copy(lgT[:, :], pb[0:NE, 0:S]).then_inc(lgT_ready, 1)
                dve.wait_ge(logits_tp, 1)
                link(dve.tensor_copy(lg, pa[:, 0:16]))
                other = te(lg).unsqueeze(2).broadcast_to([P, NT, NE, NE])
                own = te(lg).unsqueeze(3).broadcast_to([P, NT, NE, NE])
                lower = before.unsqueeze(1).broadcast_to([P, NT, NE, NE])
                dve.tensor_tensor(big, other, own, ALU.is_gt)
                link(dve.tensor_tensor(big2, other, own, ALU.is_equal))
                for t in range(NT):
                    ins = dve.tensor_tensor(big2[:, t], big2[:, t], before, ALU.mult)
                link(ins)
                link(dve.tensor_tensor(f(256, 128), f(256, 128), f(384, 128), ALU.add))
                dve.tensor_reduce(te(rank), big, AX.X, ALU.add)
                link(dve.tensor_reduce(m1, te(lg), AX.X, ALU.max))
                dve.tensor_scalar(sel, rank, 1.5, None, ALU.is_lt).then_inc(sel_ready, 1)
                dve.tensor_tensor(te(sh), te(lg), m1.unsqueeze(2).broadcast_to([P, NT, NE]),
                                  ALU.subtract).then_inc(lshift_ready, 1)
                dve.wait_ge(sel_ready, 1)
                dve.wait_ge(lexp_done, 1)
                link(dve.tensor_tensor(ex, ex, sel, ALU.mult))
                link(dve.tensor_reduce(den, te(ex), AX.X, ALU.add))
                link(dve.reciprocal(den, den))
                link(dve.tensor_tensor(te(gates), te(ex), den.unsqueeze(2).broadcast_to([P, NT, NE]), ALU.mult))
                dve.wait_ge(count_done, 1)
                link(dve.scalar_tensor_tensor(out=pos, in0=pb[:, C4:C4 + 16], scalar=1.0, in1=sel,
                                              op0=ALU.add, op1=ALU.mult))
                link(dve.tensor_scalar(pos, pos, -1.0, None, ALU.add))
                dve.tensor_copy(item_pos[:, :, 0:NE], te(pos))
                dve.wait_ge(count_done, 2)
                dve.tensor_copy(cnt, pa[:, 16:24])
                dve.tensor_copy(item_gate[:, :, 0:NE], te(gates)).then_inc(slots_ready, 1)
                dve.wait_ge(slots_ready, 1)
                make_picks(0)

            def expert_split(i, k):
                seq, c = MOE0 + k // 2, k % 2
                dve.wait_ge(hi_ready, i * PH + MH + k + 1)
                src, hi, lo = halves(seq, EXPERT[k // 2][0] == "down")[c]
                dve.tensor_tensor(lo, src, hi.bitcast(F32), ALU.subtract).then_inc(split_ready, 1)

            def make_picks(i):
                at = bass.ds(i, 1)
                dve.tensor_copy(cur[:, 0, :], item_pos[:, :, at].rearrange("p t i -> p (t i)"))
                dve.tensor_copy(cur[:, 1, :], item_gate[:, :, at].rearrange("p t i -> p (t i)")).then_inc(cur_ready, 1)
                dve.wait_ge(cur_ready, i + 1)
                for t in range(NT):
                    dve.tensor_scalar(pick[:, t, :], iota, cur[:, 0, t:t + 1], None, ALU.is_equal)
                    ins = dve.tensor_scalar(gpick[:, t, :], iota, cur[:, 0, t:t + 1], cur[:, 1, t:t + 1],
                                            ALU.is_equal, ALU.mult)
                ins.then_inc(pick_ready, 1)

            def tokens_gathered(i):
                dve.wait_ge(gather_done, i + 1)
                dve.tensor_copy(xnat[0:CAP, 0:C4], pa[0:CAP, 0:C4]).then_inc(xnat_dve, 1)

            def tokens_in(i):
                dve.wait_ge(xT_hi_ready, i + 1)
                dve.tensor_tensor(xT_lo[:, :, :].rearrange("p (b t) n -> p b (t n)", b=2),
                                  pa[:, :].rearrange("p (b n) -> p b n", b=2)[:, :, 0:4 * CAP],
                                  xT_hi[:, :, :].rearrange("p (b t) n -> p b (t n)", b=2).bitcast(F32),
                                  ALU.subtract).then_inc(xT_ready, 1)

            def combined(i, t):
                for j in range(2):
                    q = facc[:, t, j * C4:(j + 1) * C4]
                    dve.wait_ge(comb_done, i * 4 + 2 * t + j + 1)
                    dve.wait_ge(facc_done, i * 4 + 2 * t + j + 1)
                    dve.tensor_tensor(q, q, pa[:, j * C4:(j + 1) * C4], ALU.add).then_inc(facc_done, 1)

            def expert_pass(i, first, last):
                ahead = [first]

                def split_until(k):
                    while ahead[0] < min(k, last):
                        if ahead[0] < PH:
                            expert_split(i, ahead[0])
                        else:
                            expert_split(i + 1, ahead[0] - PH)
                        ahead[0] += 1

                def hidden_turned(b):
                    dve.wait_ge(eT_hi_ready, i * EBLOCKS + b + 1)
                    dve.tensor_tensor(eT_lo[:, b % 2].rearrange("p f n -> p (f n)"), pb[:, 0:4 * CAP],
                                      eT_hi[:, b % 2].rearrange("p f n -> p (f n)").bitcast(F32),
                                      ALU.subtract).then_inc(eT_ready, 1)

                for j, (what, b) in enumerate(EXPERT):
                    for c in range(2):
                        k = 2 * j + c
                        split_until(k + 3)
                        if what == "gate" and c == 0 and b:
                            hidden_turned(b - 1)
                        if (what, b, c) == ("down", EBLOCKS - 2, 0):
                            hidden_turned(EBLOCKS - 1)
                        if (what, b, c) == ("gate", 0, 1):
                            combined(i, 0)
                        if (what, b, c) == ("up", 0, 0):
                            combined(i, 1)
                        if what == "up" and c == 1:
                            dve.wait_ge(half_done, i * PH + MH + k + 1)
                            dve.wait_ge(esilu_ready, i * EBLOCKS + b + 1)
                            dve.tensor_tensor(ehid[0:CAP, :], ehid[0:CAP, :], pc[0:CAP, C4:2 * C4],
                                              ALU.mult).then_inc(ehid_ready, 1)
                            if b == 0:
                                dve.wait_ge(spread_tp, i + 1)
                                make_picks(i + 1)
                        if (what, b, c) == ("down", 2, 1):
                            tokens_gathered(i + 1)
                        if (what, b, c) == ("up", EBLOCKS - 1, 1):
                            tokens_in(i + 1)
                dve.wait_ge(half_done, i * PH + MH + PH)
                dve.tensor_copy(ynat[0:CAP, 0:C4], pd[0:CAP, 0:C4]).then_inc(ynat_dve, 1)
                split_until(PH + 3)

            pre_norm(0)
            mixing(0)
            post_norm(0, 2 * MIX_LOADS)
            pre_norm(1)
            dense()
            post_norm(1, 2 * (MIX_LOADS + DENSE_LOADS))
            pre_norm(2)
            mixing(1)
            post_norm(2, MH)
            pre_norm(3)
            expert_split(0, 0)
            routing()
            expert_split(0, 1)
            expert_split(0, 2)
            tokens_gathered(0)
            tokens_in(0)
            with dve.Fori(0, NE - 1) as i:
                expert_pass(i, 3, PH + 3)
            dve.wait_ge(plan_ready, 1)
            expert_pass(NE - 1, 3, PH)
            extra = dve.value_load(plan[0:1, 7:8], min_val=0, max_val=EXTRA)
            with dve.Fori(0, EXTRA) as n:
                with dve.If(n < extra):
                    expert_pass(n + NE, 0, PH)
            for t in range(NT):
                combined(extra + NE, t)
            post_norm(3, extra * 4 + 4 * NE + 4)


_INS = ['x', 'mix_norm_pre', 'mix_norm_post', 'ffn_norm_pre', 'ffn_norm_post', 'w_in', 'pool_w', 'pool_scale',
        'na_rpb', 'w_out', 'dense_w_gate', 'dense_w_up', 'dense_w_down', 'moe_router', 'moe_w_gate', 'moe_w_up',
        'moe_w_down']


def shape_constants():
    import numpy as np
    c = np.zeros((P, K_ALL), np.float32)
    p = np.arange(P)
    c[:, K_ID:K_ID + P] = np.eye(P)
    c[:, K_TRI:K_TRI + P] = p[:, None] < p[None, :]
    c[:, K_ONE:K_ONE + P] = 1
    c[:, K_IOTA:K_IOTA + CAP] = np.arange(CAP)
    for b in range(2):
        first = np.clip(QC - 1 - p % QC + QC * b - KWIN // 2, 0, COLS - KWIN)[:, None]
        col = WIN0 * b + np.arange(WIN)[None, :]
        seen = (col >= first) & (col < first + KWIN)
        c[:, K_MASK + b * WIN:K_MASK + (b + 1) * WIN] = np.where(seen, 0, MASKED)
    t = np.concatenate([np.arange(8), np.arange(S - 8, S)])
    for g in range(4):
        w = 2 << g
        n = np.clip(t + w - w // 2, 0, S) - np.clip(t - w // 2, 0, S)
        c[:, K_EDGE + 16 * g:K_EDGE + 16 * (g + 1)] = w / n
    e = np.arange(NE)
    c[:, K_EPS] = EPS
    c[:, K_LT:K_LT + 64] = (e[None, :] < e[:, None]).reshape(-1)
    return c


def kernel(**inputs):
    import numpy as np
    import concourse.bacc as bacc
    from concourse.bass_utils import run_bass_kernel_spmd

    nc = bacc.Bacc("TRN2", target_bir_lowering=False, num_devices=1)
    arrays, args = {}, []
    for name in _INS:
        a = np.ascontiguousarray(inputs[name])
        arrays[f"in_{name}"] = a
        args.append(nc.dram_tensor(f"in_{name}", a.shape, mybir.dt.from_np(a.dtype), kind="ExternalInput").ap())
    consts = shape_constants()
    arrays["in_consts"] = consts
    args.append(nc.dram_tensor("in_consts", consts.shape, F32, kind="ExternalInput").ap())
    args.append(nc.dram_tensor("out", (1, S, D), F32, kind="ExternalOutput").ap())
    hybrid_encoder(nc, *args)
    r = run_bass_kernel_spmd(nc, [arrays], core_ids=[0])
    return r.results[0]["out"]
```
